# Optimizing a Trainium2 kernel written in Bass

```python
import jax, jax.numpy as jnp
from jax import lax
import numpy as np

D_MODEL = 1024
BATCH = 1
SEQ = 512
DEPTH = 1

CHUNK = 64
CONV_W = D_MODEL
CONV_A_K = 3
LRU_W = D_MODEL
LRU_HEADS = 8
LRU_BW = LRU_W // LRU_HEADS
CONV_B_K = 4
LRU_C = 8.0
D_FF = 4 * D_MODEL
N_MOD = 6
N_IN = 3 * CONV_W + 2 * LRU_W + 2 * D_MODEL
EPS = 1e-6
SPLITS = (CONV_W, 2 * CONV_W, 3 * CONV_W, 3 * CONV_W + LRU_W,
          3 * CONV_W + 2 * LRU_W, 3 * CONV_W + 2 * LRU_W + D_MODEL)

kernel_name = "hybrid_shortconv_rglru_sandwich_adaln"

def rms_norm(x, g):
    xf = x.astype(jnp.float32)
    y = xf * lax.rsqrt(jnp.mean(xf * xf, axis=-1, keepdims=True) + EPS)
    return (y * g.astype(jnp.float32)).astype(x.dtype)

def causal_dwconv(x, w, b):
    k_w = w.shape[0]
    s = x.shape[1]
    xp = jnp.pad(x, ((0, 0), (k_w - 1, 0), (0, 0)))
    y = b
    for k in range(k_w):
        y = y + xp[:, k:k + s, :] * w[k]
    return y

def block_diag_linear(x, w, b):
    bsz, s, _ = x.shape
    xh = x.reshape(bsz, s, LRU_HEADS, LRU_BW)
    y = jnp.einsum("bshi,hij->bshj", xh, w).reshape(bsz, s, LRU_W)
    return y + b

def _lin_combine(left, right):
    a1, b1 = left
    a2, b2 = right
    return a1 * a2, a2 * b1 + b2

def chunked_linear_scan(a, b):
    bsz, s, w = a.shape
    n = s // CHUNK
    a_c = a.reshape(bsz, n, CHUNK, w)
    b_c = b.reshape(bsz, n, CHUNK, w)
    a_cum, h_loc = lax.associative_scan(_lin_combine, (a_c, b_c), axis=2)

    def step(h_prev, inp):
        a_k, h_k = inp
        h_full = h_k + a_k * h_prev[:, None, :]
        return h_full[:, -1, :], h_full

    h0 = jnp.zeros((bsz, w), a.dtype)
    _, hs = lax.scan(step, h0, (jnp.swapaxes(a_cum, 0, 1), jnp.swapaxes(h_loc, 0, 1)))
    return jnp.swapaxes(hs, 0, 1).reshape(bsz, s, w)

def rg_lru(x, w_r, b_r, w_i, b_i, lam):
    xf = x.astype(jnp.float32)
    r = jax.nn.sigmoid(block_diag_linear(xf, w_r.astype(jnp.float32), b_r.astype(jnp.float32)))
    i = jax.nn.sigmoid(block_diag_linear(xf, w_i.astype(jnp.float32), b_i.astype(jnp.float32)))
    log_a = -LRU_C * r * jax.nn.softplus(-lam.astype(jnp.float32))
    a = jnp.exp(log_a)
    mult = jnp.sqrt(-jnp.expm1(2.0 * log_a))
    h = chunked_linear_scan(a, mult * (i * xf))
    return h.astype(x.dtype)

def hybrid_mixer(h, w_in, conv_a_w, conv_a_b, w_a_out, conv_b_w, conv_b_b,
                 w_gate_r, b_gate_r, w_gate_i, b_gate_i, lru_lambda, w_b_out, w_o):
    proj = h @ w_in
    b_a, c_a, v_a, x_b, g_b, u_a, u_b = jnp.split(proj, SPLITS, axis=-1)
    y_a = b_a * causal_dwconv(c_a * v_a, conv_a_w, conv_a_b)
    x_b = causal_dwconv(x_b, conv_b_w, conv_b_b)
    y_b = rg_lru(x_b, w_gate_r, b_gate_r, w_gate_i, b_gate_i, lru_lambda) * jax.nn.gelu(g_b)
    m = jax.nn.sigmoid(u_a) * (y_a @ w_a_out) + jax.nn.sigmoid(u_b) * (y_b @ w_b_out)
    return m @ w_o

def sq_relu_mlp(h, w_up, w_down):
    return jnp.square(jax.nn.relu(h @ w_up)) @ w_down

def setup_inputs(seed: int = 0) -> dict:
    key = jax.random.key(seed)
    ks = jax.random.split(key, 24)
    L, D = DEPTH, D_MODEL
    f32 = jnp.float32

    def nrm(k, shape, scale):
        return jax.random.normal(k, shape, f32) * scale

    u = jax.random.uniform(ks[15], (L, LRU_W), f32, 0.9, 0.999)
    return {
        "x": nrm(ks[0], (BATCH, SEQ, D), 1.0),
        "c": nrm(ks[1], (BATCH, D), 1.0),
        "w_mod": nrm(ks[2], (L, D, N_MOD * D), 0.5 * D ** -0.5),
        "b_mod": nrm(ks[3], (L, N_MOD * D), 0.02),
        "g_pre_mix": 1.0 + nrm(ks[4], (L, D), 0.02),
        "g_post_mix": 1.0 + nrm(ks[5], (L, D), 0.02),
        "w_in": nrm(ks[6], (L, D, N_IN), D ** -0.5),
        "conv_a_w": nrm(ks[7], (L, CONV_A_K, CONV_W), CONV_A_K ** -0.5),
        "conv_a_b": nrm(ks[8], (L, CONV_W), 0.02),
        "w_a_out": nrm(ks[9], (L, CONV_W, D), CONV_W ** -0.5),
        "conv_b_w": nrm(ks[10], (L, CONV_B_K, LRU_W), CONV_B_K ** -0.5),
        "conv_b_b": nrm(ks[11], (L, LRU_W), 0.02),
        "w_gate_r": nrm(ks[12], (L, LRU_HEADS, LRU_BW, LRU_BW), LRU_BW ** -0.5),
        "b_gate_r": nrm(ks[13], (L, LRU_W), 0.02),
        "w_gate_i": nrm(ks[14], (L, LRU_HEADS, LRU_BW, LRU_BW), LRU_BW ** -0.5),
        "b_gate_i": nrm(ks[16], (L, LRU_W), 0.02),
        "lru_lambda": jnp.log(u) - jnp.log1p(-u),
        "w_b_out": nrm(ks[17], (L, LRU_W, D), LRU_W ** -0.5),
        "w_o": nrm(ks[18], (L, D, D), D ** -0.5),
        "g_pre_mlp": 1.0 + nrm(ks[19], (L, D), 0.02),
        "g_post_mlp": 1.0 + nrm(ks[20], (L, D), 0.02),
        "w_mlp_up": nrm(ks[21], (L, D, D_FF), D ** -0.5),
        "w_mlp_down": nrm(ks[22], (L, D_FF, D), D_FF ** -0.5),
    }

def reference(x, c, w_mod, b_mod, g_pre_mix, g_post_mix, w_in, conv_a_w, conv_a_b,
              w_a_out, conv_b_w, conv_b_b, w_gate_r, b_gate_r, w_gate_i, b_gate_i,
              lru_lambda, w_b_out, w_o, g_pre_mlp, g_post_mlp, w_mlp_up, w_mlp_down):
    c_act = jax.nn.silu(c)
    for l in range(DEPTH):
        mod = (c_act @ w_mod[l] + b_mod[l])[:, None, :]
        sh_m, sc_m, gt_m, sh_f, sc_f, gt_f = jnp.split(mod, N_MOD, axis=-1)
        h = rms_norm(x, g_pre_mix[l]) * (1.0 + sc_m) + sh_m
        y = hybrid_mixer(h, w_in[l], conv_a_w[l], conv_a_b[l], w_a_out[l],
                         conv_b_w[l], conv_b_b[l], w_gate_r[l], b_gate_r[l],
                         w_gate_i[l], b_gate_i[l], lru_lambda[l], w_b_out[l], w_o[l])
        x = x + gt_m * rms_norm(y, g_post_mix[l])
        h = rms_norm(x, g_pre_mlp[l]) * (1.0 + sc_f) + sh_f
        y = sq_relu_mlp(h, w_mlp_up[l], w_mlp_down[l])
        x = x + gt_f * rms_norm(y, g_post_mlp[l])
    return x


_drawn_inputs = setup_inputs


def setup_inputs(seed=0):
    import zlib

    import numpy as np

    out = dict(_drawn_inputs(seed))
    spreads = {}
    factors = {'g_pre_mix': 5.911,
     'g_post_mix': 8.0,
     'conv_a_b': 64.0,
     'conv_b_b': 64.0,
     'b_gate_r': 200.0,
     'b_gate_i': 200.0,
     'g_pre_mlp': 28.139,
     'g_post_mlp': 104.964}
    for name, (base, spread) in spreads.items():
        noise = np.random.default_rng([zlib.crc32(name.encode()), seed]).standard_normal(out[name].shape)
        drawn = base * np.exp(spread * noise) if base else spread * noise
        out[name] = __import__('jax').numpy.asarray(drawn.astype(out[name].dtype))
    for name, factor in factors.items():
        out[name] = (out[name] * factor).astype(out[name].dtype)
    return out
```

```python
import concourse.bass as bass
from concourse import mybir
from contextlib import ExitStack


def hybrid_layer_kernel(nc, x, c, w_mod, b_mod, g_pre_mix, g_post_mix, w_in, conv_a_w, conv_a_b,
                        w_a_out, conv_b_w, conv_b_b, w_gate_r, b_gate_r, w_gate_i, b_gate_i,
                        lru_lambda, w_b_out, w_o, g_pre_mlp, g_post_mlp, w_mlp_up, w_mlp_down, out):
    f32 = mybir.dt.float32
    f32r = mybir.dt.float32r
    ALU = mybir.AluOpType
    ACT = mybir.ActivationFunctionType
    AX = mybir.AxisListType
    ds = bass.ds

    P = 128
    SEQ, D = x.shape[1], x.shape[2]
    NB = D // P
    TB = SEQ // P
    FB = w_mlp_up.shape[2] // P
    HALF = D // 2
    KA, KB = conv_a_w.shape[1], conv_b_w.shape[1]
    EPS = 1e-6
    LRU_C = 8.0
    RING = 4
    U_MIX, U_GATE, U_BOUT, U_WO, U_UP = 0, 4 * NB, 8 * NB, 9 * NB, 10 * NB
    U_DOWN = U_UP + FB
    U_END = U_DOWN + FB

    w_in_v = w_in[0].rearrange("(k p) n -> p k n", p=P)
    w_a_v = w_a_out[0].rearrange("(k p) n -> p k n", p=P)
    w_b_v = w_b_out[0].rearrange("(k p) n -> p k n", p=P)
    w_o_v = w_o[0].rearrange("(k p) n -> p k n", p=P)
    w_up_v = w_mlp_up[0].rearrange("(k p) n -> p k n", p=P)
    w_dn_v = w_mlp_down[0].rearrange("(k p) n -> p k n", p=P)
    w_mod_v = w_mod[0].rearrange("(k p) n -> p k n", p=P)
    x_v = x[0].rearrange("(t p) d -> p t d", p=P)
    out_v = out[0].rearrange("(t p) d -> p t d", p=P)
    COL_B, COL_C, COL_V, COL_XB, COL_G, COL_UA, COL_UB = [j * D for j in range(7)]

    ctx = ExitStack()
    with ctx:
        def sem(name):
            return ctx.enter_context(nc.semaphore(name))

        def sb(name, shape, dt=f32):
            return ctx.enter_context(nc.sbuf_tensor(name, shape, dt))

        ident = sb("ident", [P, P])
        ones = sb("ones", [P, P])
        cols = sb("cols", [P, P])
        s_mix = sb("s_mix", [P, NB])
        s_mlp = sb("s_mlp", [P, NB])
        mcol = sb("mcol", [P, 4 * NB])
        c_act = sb("c_act", [P, NB])
        k_neg = sb("k_neg", [P, NB])
        k_pos = sb("k_pos", [P, NB])
        sp = sb("sp", [P, 6, NB])
        stat = sb("stat", [P, 16])
        eps_t = sb("eps_t", [P, 1])

        KIB = 1024
        ROW = SEQ * 4
        base = (nc.sbuf_base + 31) // 32 * 32
        room = nc.sbuf_usable_end - base - 512
        arena_bytes = 204 * KIB
        assert arena_bytes <= room, (arena_bytes, room)
        arena = ctx.enter_context(nc.sbuf_tensor("arena", [P, arena_bytes // 4], f32))
        O_XS, O_HT, O_YA, O_YB, O_RING, O_RAW, O_HM, O_MB, O_MR, O_GS = [
            base + KIB * k for k in (0, 16, 48, 80, 112, 144, 160, 176, 192, 200)]

        def at(name, shape, off, dt=f32):
            return nc.alloc_sbuf_tensor_at(name, shape, dt, offset=off)

        xs = at("xs", [P, TB, D], O_XS)
        sig_b = at("sig_b", [P, NB, SEQ], O_XS)
        ht_hi = at("ht_hi", [P, NB, SEQ], O_HT, f32r)
        ht_lo = at("ht_lo", [P, NB, SEQ], O_HT + 16 * KIB, f32r)
        wo2_hi = at("wo2_hi", [P, RING, D], O_HT, f32r)
        wo2_lo = at("wo2_lo", [P, RING, D], O_HT + 16 * KIB, f32r)
        ya_hi = at("ya_hi", [P, NB, SEQ], O_YA, f32r)
        ya_lo = at("ya_lo", [P, NB, SEQ], O_YA + 16 * KIB, f32r)
        m_hi = at("m_hi", [P, NB, SEQ], O_YA, f32r)
        m_lo = at("m_lo", [P, NB, SEQ], O_YA + 16 * KIB, f32r)
        hid = at("hid", [P, FB, SEQ], O_HT)
        yb_hi = at("yb_hi", [P, NB, SEQ], O_YB, f32r)
        yb_lo = at("yb_lo", [P, NB, SEQ], O_YB + 16 * KIB, f32r)
        h2_hi = at("h2_hi", [P, NB, SEQ], O_YB, f32r)
        h2_lo = at("h2_lo", [P, NB, SEQ], O_YB + 16 * KIB, f32r)
        w_hi = at("w_hi", [P, RING, D], O_RING, f32r)
        w_lo = at("w_lo", [P, RING, D], O_RING + 16 * KIB, f32r)
        raw = at("raw", [P, RING, D], O_RAW)
        xnt = at("xnt", [P, NB, SEQ], O_HM)
        hm = at("hm", [P, NB, SEQ], O_HM)
        modb = at("modb", [P, 4 * D], O_MB)
        modraw = at("modraw", [P, 2, 2, HALF], O_MR)
        g_bc = at("g_bc", [P, 2, D], O_MR)
        gel = at("gel", [P, SEQ], O_GS)
        sig_a = at("sig_a", [P, SEQ], O_GS + ROW)
        dtmp = at("dtmp", [P, D], O_GS)
        mod0_raw = at("mod0_raw", [P, 2, 2 * D], O_YB)
        mod0 = at("mod0", [P, 2 * D], O_YB + 16 * KIB)
        vrows = at("vrows", [P, P], O_YB + 24 * KIB)
        xc, xc_hi, xc_lo, c_sb, ca, r_t, i_t, t_t, a_t, q_t = [
            at(nm, [P, SEQ], O_YB + ROW * k, f32r if nm in ("xc_hi", "xc_lo") else f32)
            for k, nm in enumerate("xc xc_hi xc_lo c_sb ca r_t i_t t_t a_t q_t".split())]
        g_hi = at("g_hi", [P, 2, P], O_YB + 20 * KIB, f32r)
        g_lo = at("g_lo", [P, 2, P], O_YB + 21 * KIB, f32r)
        graw = at("graw", [P, 2, P], O_YB + 22 * KIB)
        xbp = at("xbp", [P, KB - 1 + SEQ], O_YB + 25 * KIB)
        cvp = at("cvp", [P, KA - 1 + SEQ], O_YB + 28 * KIB)
        y1 = at("y1", [P, D], O_HM)
        xn2 = at("xn2", [P, D], O_HM + 4 * KIB)
        h2f = at("h2f", [P, NB, P], O_HM + 8 * KIB)
        junk = at("junk", [P, D], O_HM + 12 * KIB)
        junk0 = at("junk0", [P, D], O_GS)
        relu_t = at("relu_t", [P, 2, SEQ], O_GS)
        hd_hi = at("hd_hi", [P, RING, SEQ], O_HM, f32r)
        hd_lo = at("hd_lo", [P, RING, SEQ], O_HM + 8 * KIB, f32r)
        y2 = at("y2", [P, D], O_MR)
        junk2 = at("junk2", [P, D], O_GS)

        ps = ctx.enter_context(nc.psum_tensor("ps", [P, 8, HALF], f32))
        B_R, B_I, B_T0, B_T1 = 4, 5, 6, 7

        C_C, C_GX, C_GM, C_AW, C_AB, C_BW = 0, NB, 2 * NB, 3 * NB, (3 + KA) * NB, (4 + KA) * NB
        C_BB = C_BW + KB * NB
        C_BR, C_BI, C_LAM = C_BB + NB, C_BB + 2 * NB, C_BB + 3 * NB
        NCOL = C_LAM + NB
        vectors = [(C_C, c[0]), (C_GX, g_pre_mix[0]), (C_GM, g_pre_mlp[0]), (C_AB, conv_a_b[0]),
                   (C_BB, conv_b_b[0]), (C_BR, b_gate_r[0]), (C_BI, b_gate_i[0]), (C_LAM, lru_lambda[0])]

        raw_in0 = sem("raw_in0")
        raw_in1 = sem("raw_in1")
        raw_in2 = sem("raw_in2")
        raw_in3 = sem("raw_in3")
        graw_in = sem("graw_in")
        loads_begun = sem("loads_begun")
        vec_in = sem("vec_in")
        xr_in0 = sem("xr_in0")
        xr_in1 = sem("xr_in1")
        xr_in2 = sem("xr_in2")
        xr_in3 = sem("xr_in3")
        mod0_in0 = sem("mod0_in0")
        mod0_in1 = sem("mod0_in1")
        modraw_in0 = sem("modraw_in0")
        modraw_in1 = sem("modraw_in1")
        bmod0_in = sem("bmod0_in")
        bmod_in = sem("bmod_in")
        gbc_in = sem("gbc_in")
        out_done = sem("out_done")
        const_ready = sem("const_ready")
        zero0_ready = sem("zero0_ready")
        zeromb_ready = sem("zeromb_ready")
        cols_sum = sem("cols_sum")
        cols_ready = sem("cols_ready")
        cact = sem("cact")
        sig_c = sem("sig_c")
        sp_act = sem("sp_act")
        sp_step = sem("sp_step")
        mod0_acc = sem("mod0_acc")
        mod0_sum = sem("mod0_sum")
        diag_step = sem("diag_step")
        col0_ready = sem("col0_ready")
        h_f32 = sem("h_f32")
        h_hi = sem("h_hi")
        h_lo = sem("h_lo")
        x_sq = sem("x_sq")
        x_var = sem("x_var")
        x_sqrt = sem("x_sqrt")
        x_rstd = sem("x_rstd")
        x_norm = sem("x_norm")
        x_tr = sem("x_tr")
        xnt_ready = sem("xnt_ready")
        w_hi_ready = sem("w_hi_ready")
        w_lo_ready = sem("w_lo_ready")
        unit_done = sem("unit_done")
        gates_done = sem("gates_done")
        xb_copied = sem("xb_copied")
        xc_tap = sem("xc_tap")
        xc_conv = sem("xc_conv")
        xc_hi_ready = sem("xc_hi_ready")
        xc_lo_ready = sem("xc_lo_ready")
        c_copied = sem("c_copied")
        cv_ready = sem("cv_ready")
        ca_tap = sem("ca_tap")
        ca_conv = sem("ca_conv")
        ya_f32 = sem("ya_f32")
        ya_hi_ready = sem("ya_hi_ready")
        ya_lo_ready = sem("ya_lo_ready")
        g_hi_ready = sem("g_hi_ready")
        g_lo_ready = sem("g_lo_ready")
        r_ready = sem("r_ready")
        i_ready = sem("i_ready")
        t_ready = sem("t_ready")
        a_ready = sem("a_ready")
        q_ready = sem("q_ready")
        q2_ready = sem("q2_ready")
        mult_ready = sem("mult_ready")
        ix_ready = sem("ix_ready")
        bx_ready = sem("bx_ready")
        scan_ready = sem("scan_ready")
        gelu_ready = sem("gelu_ready")
        yb_f32 = sem("yb_f32")
        yb_hi_ready = sem("yb_hi_ready")
        yb_lo_ready = sem("yb_lo_ready")
        siga_ready = sem("siga_ready")
        m_part = sem("m_part")
        sigb_ready = sem("sigb_ready")
        mod_acc = sem("mod_acc")
        mod_sum = sem("mod_sum")
        mod_copied = sem("mod_copied")
        gm_ready = sem("gm_ready")
        colf_ready = sem("colf_ready")
        bout_scaled = sem("bout_scaled")
        m_f32 = sem("m_f32")
        m_hi_ready = sem("m_hi_ready")
        m_lo_ready = sem("m_lo_ready")
        y_done = sem("y_done")
        y_sq = sem("y_sq")
        y_var = sem("y_var")
        y_sqrt = sem("y_sqrt")
        y_rstd = sem("y_rstd")
        y_scaled = sem("y_scaled")
        x1_ready = sem("x1_ready")
        x1_sq = sem("x1_sq")
        x1_var = sem("x1_var")
        x1_sqrt = sem("x1_sqrt")
        x1_rstd = sem("x1_rstd")
        xn2_ready = sem("xn2_ready")
        xn2_tr = sem("xn2_tr")
        h2_f32 = sem("h2_f32")
        h2_hi_ready = sem("h2_hi_ready")
        h2_lo_ready = sem("h2_lo_ready")
        relu_ready = sem("relu_ready")
        hid_ready = sem("hid_ready")
        hd_hi_ready = sem("hd_hi_ready")
        hd_lo_ready = sem("hd_lo_ready")
        z_done = sem("z_done")
        z_sq = sem("z_sq")
        z_var = sem("z_var")
        z_sqrt = sem("z_sqrt")
        z_rstd = sem("z_rstd")
        z_scaled = sem("z_scaled")
        z_out = sem("z_out")
        raw_in = [raw_in0, raw_in1, raw_in2, raw_in3]
        xr_in = [xr_in0, xr_in1, xr_in2, xr_in3]
        mod0_in = [mod0_in0, mod0_in1]
        modraw_in = [modraw_in0, modraw_in1]

        def wait(eng, semaphore, count):
            if not isinstance(count, int) or count > 0:
                eng.wait_ge(semaphore, count)

        def mm3(dst, l_hi, l_lo, r_hi, r_lo, first, last):
            nc.tensor.matmul(dst, l_hi, r_hi, start=first, stop=False)
            nc.tensor.matmul(dst, l_hi, r_lo, start=False, stop=False)
            return nc.tensor.matmul(dst, l_lo, r_hi, start=False, stop=last)

        block = ctx.enter_context(nc.Block())

        @block.sync
        def _(sp_eng):
            def load_unit(u, slot, src):
                wait(sp_eng, w_lo_ready, u - RING + 1)
                sp_eng.sem_inc(loads_begun, 1)
                dst = raw[:, slot, :]
                if len(src.shape) == 3:
                    dst = dst.rearrange("p (k n) -> p k n", k=NB)
                sp_eng.dma_start(dst, src).then_inc(raw_in[slot], 16)

            def load_gates(n):
                wait(sp_eng, g_lo_ready, n)
                sp_eng.dma_start(graw[:, 0, :], w_gate_r[0, ds(n, 1)].rearrange("a p j -> p (a j)")).then_inc(graw_in, 16)
                sp_eng.dma_start(graw[:, 1, :], w_gate_i[0, ds(n, 1)].rearrange("a p j -> p (a j)")).then_inc(graw_in, 16)

            for t in range(TB):
                sp_eng.dma_start(xs[:, t, :], x_v[:, t, :]).then_inc(xr_in[t], 16)
            for k in range(NB):
                wait(sp_eng, mod0_acc, k - 1)
                sp_eng.dma_start(mod0_raw[:, k % 2, :], w_mod_v[:, k, 0:2 * D]).then_inc(mod0_in[k % 2], 16)
                if k >= NB - RING:
                    j = k - (NB - RING)
                    load_unit(j, j, w_in_v[:, :, [COL_XB, COL_C, COL_V, COL_B][j]:][:, :, 0:P])

            sp_eng.wait_ge(mod0_sum, 4)
            load_gates(0)

            with sp_eng.Fori(1, NB) as n:
                for j, col in enumerate((COL_XB, COL_C, COL_V, COL_B)):
                    load_unit(4 * n + j, j, w_in_v[:, :, ds(col + n * P, P)])
                load_gates(n)

            gate_cols = ((w_in_v, COL_G), (w_in_v, COL_UA), (w_a_v, 0), (w_in_v, COL_UB))
            b_cols = tuple((w_b_v, j * P) for j in range(RING))
            for j, (view, col) in enumerate(gate_cols):
                load_unit(U_GATE + j, j, view[:, :, ds(col, P)])

            def mod_and_next(n, nxt, nxt_cols):
                for j, (view, col) in enumerate(nxt_cols):
                    wait(sp_eng, mod_acc, 8 * n + 2 * j - 2)
                    sp_eng.sem_inc(loads_begun, 1)
                    sp_eng.dma_start(modraw[:, j % 2, :, :],
                                     w_mod_v[:, 2 * j:2 * j + 2, ds(2 * D + n * HALF, HALF)]).then_inc(modraw_in[j % 2], 16)
                    load_unit(U_GATE + 4 * n + 4 + j, j, view[:, :, ds(col + nxt * P, P)])

            mod_and_next(0, 1, gate_cols)
            with sp_eng.Fori(1, NB - 1) as n:
                mod_and_next(n, n + 1, gate_cols)
            mod_and_next(NB - 1, 0, b_cols)
            for j in range(RING):
                load_unit(U_BOUT + RING + j, j, w_b_v[:, :, (RING + j) * P:(RING + j + 1) * P])
            sp_eng.wait_ge(mod_acc, 8 * NB)
            sp_eng.dma_start(g_bc[:, 0, :], g_post_mix[0:1, :].to_broadcast([P, D])).then_inc(gbc_in, 16)
            sp_eng.dma_start(g_bc[:, 1, :], g_post_mlp[0:1, :].to_broadcast([P, D])).then_inc(gbc_in, 16)
            for k in range(NB):
                load_unit(U_WO + k, k % RING, w_o_v[:, k, :])
            sp_eng.wait_ge(m_f32, NB)
            for t in range(TB):
                sp_eng.dma_start(xs[:, t, :], x_v[:, t, :]).then_inc(xr_in[t], 16)

            with sp_eng.Fori(0, FB // RING) as q:
                for j in range(RING):
                    load_unit(U_UP + RING * q + j, j, w_up_v[:, :, ds((RING * q + j) * P, P)])
            with sp_eng.Fori(0, FB // RING) as q:
                for j in range(RING):
                    load_unit(U_DOWN + RING * q + j, j, w_dn_v[:, ds(RING * q + j, 1), :].rearrange("p a n -> p (a n)"))
            for t in range(TB):
                for h in range(2):
                    sp_eng.wait_ge(z_out, 2 * t + h + 1)
                    sp_eng.dma_start(out_v[:, t, h * HALF:(h + 1) * HALF],
                                     xs[:, t, h * HALF:(h + 1) * HALF]).then_inc(out_done, 16)
            sp_eng.wait_ge(out_done, 16 * 2 * TB)

        @block.gpsimd
        def _(pool):
            nc.gpsimd.memset(mod0[:, :], 0.0).then_inc(zero0_ready, 1)
            pool.wait_ge(zero0_ready, 1)
            pool.dma_start(mod0[0:1, :], b_mod[0:1, 0:2 * D]).then_inc(bmod0_in, 16)
            nc.gpsimd.memset(ident[:, :], 0.0).then_inc(const_ready, 1)
            pool.wait_ge(const_ready, 1)
            nc.gpsimd.affine_select(out=ident[:, :], in_=ident[:, :], compare_op=ALU.not_equal, fill=1.0,
                                    base=0, pattern=[[-1, P]], channel_multiplier=1).then_inc(const_ready, 1)
            nc.gpsimd.memset(ones[:, :], 1.0).then_inc(const_ready, 1)
            nc.gpsimd.memset(eps_t[:, :], EPS).then_inc(const_ready, 1)
            nc.gpsimd.memset(modb[:, :], 0.0).then_inc(zeromb_ready, 1)
            pool.wait_ge(zeromb_ready, 1)
            pool.dma_start(modb[0:1, :], b_mod[0:1, 2 * D:6 * D]).then_inc(bmod_in, 16)
            pool.wait_ge(cols_sum, 1)
            nc.gpsimd.memset(xbp[:, 0:KB - 1], 0.0).then_inc(const_ready, 1)
            nc.gpsimd.memset(cvp[:, 0:KA - 1], 0.0).then_inc(const_ready, 1)

        @block.scalar
        def _(act):
            A = nc.scalar.activation

            def split_hi(u, slot, u_free=None):
                wait(act, unit_done, u - RING + 1 if u_free is None else u_free)
                act.wait_ge(raw_in[slot], 16 * (u // RING + 1))
                A(w_hi[:, slot, :], raw[:, slot, :], ACT.Copy).then_inc(w_hi_ready, 1)

            for off, vec in vectors:
                act.dma_start(vrows[off:off + NB, :], vec.rearrange("(b p) -> b p", p=P)).then_inc(vec_in, 16)
            act.dma_start(vrows[C_AW:C_AW + KA * NB, :], conv_a_w[0].rearrange("k (b p) -> (k b) p", p=P)).then_inc(vec_in, 16)
            act.dma_start(vrows[C_BW:C_BW + KB * NB, :], conv_b_w[0].rearrange("k (b p) -> (k b) p", p=P)).then_inc(vec_in, 16)

            act.wait_ge(cols_ready, 1)
            A(c_act[:, :], cols[:, C_C:C_C + NB], ACT.Sigmoid).then_inc(sig_c, 1)
            for t in range(TB):
                act.wait_ge(xr_in[t], 16)
                wait(act, x_sq, t)
                A(junk0[:, :], xs[:, t, :], ACT.Square, accum_out=stat[:, t:t + 1]).then_inc(x_sq, 1)
            act.wait_ge(sp_step, 1)
            A(sp[:, 1, :], sp[:, 0, :], ACT.Exp).then_inc(sp_act, 1)
            act.wait_ge(x_sq, TB)
            act.wait_ge(const_ready, 4)
            A(stat[:, 4:8], stat[:, 0:4], ACT.Sqrt, scale=1.0 / D, bias=eps_t[:, 0:1]).then_inc(x_sqrt, 1)
            for k in range(NB):
                act.wait_ge(x_tr, k + 1)
                A(xnt[:, k, :], ps[:, k, :], ACT.Copy).then_inc(xnt_ready, 1)
            for j in range(RING):
                split_hi(j, j)
            for k in range(NB):
                act.wait_ge(h_f32, k + 1)
                A(ht_hi[:, k, :], xnt[:, k, :], ACT.Copy).then_inc(h_hi, 1)

            def split_gates(n):
                wait(act, gates_done, n)
                act.wait_ge(graw_in, 32 * (n + 1))
                A(g_hi[:, :, :], graw[:, :, :], ACT.Copy).then_inc(g_hi_ready, 1)

            def recurrence(n):
                act.wait_ge(gates_done, n + 1)
                A(r_t[:, :], ps[:, B_R, :], ACT.Sigmoid, bias=cols[:, ds(C_BR + n, 1)]).then_inc(r_ready, 1)
                A(i_t[:, :], ps[:, B_I, :], ACT.Sigmoid, bias=cols[:, ds(C_BI + n, 1)]).then_inc(i_ready, 1)
                act.wait_ge(r_ready, n + 1)
                A(t_t[:, :], r_t[:, :], ACT.Tanh, scale=k_pos[:, ds(n, 1)]).then_inc(t_ready, 1)
                A(a_t[:, :], r_t[:, :], ACT.Exp, scale=k_neg[:, ds(n, 1)]).then_inc(a_ready, 1)
                act.wait_ge(a_ready, n + 1)
                A(q_t[:, :], a_t[:, :], ACT.Square).then_inc(q_ready, 1)

            def recurrence_root(n):
                act.wait_ge(q2_ready, n + 1)
                A(q_t[:, :], q_t[:, :], ACT.Sqrt).then_inc(mult_ready, 1)

            def mix(n, after_xb):
                act.wait_ge(unit_done, 4 * n + 1)
                wait(act, xc_conv, 3 * n)
                A(xbp[:, KB - 1:], ps[:, 0, :], ACT.Copy).then_inc(xb_copied, 1)
                wait(act, ix_ready, n)
                A(xc[:, :], ps[:, 0, :], ACT.Identity, scale=cols[:, ds(C_BW + (KB - 1) * NB + n, 1)],
                  bias=cols[:, ds(C_BB + n, 1)]).then_inc(xc_tap, 1)
                split_hi(4 * n + 4, 0)
                after_xb()
                wait(act, gates_done, n)
                act.wait_ge(xc_conv, 3 * (n + 1))
                A(xc_hi[:, :], xc[:, :], ACT.Copy).then_inc(xc_hi_ready, 1)
                split_gates(n)
                act.wait_ge(unit_done, 4 * n + 2)
                wait(act, cv_ready, n)
                A(c_sb[:, :], ps[:, 1, :], ACT.Copy).then_inc(c_copied, 1)
                split_hi(4 * n + 5, 1)
                act.wait_ge(cv_ready, n + 1)
                wait(act, ya_lo_ready, n)
                A(ca[:, :], cvp[:, KA - 1:], ACT.Identity, scale=cols[:, ds(C_AW + (KA - 1) * NB + n, 1)],
                  bias=cols[:, ds(C_AB + n, 1)]).then_inc(ca_tap, 1)
                split_hi(4 * n + 6, 2)
                act.wait_ge(ya_f32, n + 1)
                A(ya_hi[:, ds(n, 1), :], ca[:, None, :], ACT.Copy).then_inc(ya_hi_ready, 1)
                split_hi(4 * n + 7, 3)

            act.wait_ge(const_ready, 6)
            act.wait_ge(cols_ready, 2)
            mix(0, lambda: None)
            with act.Fori(1, NB) as n:
                recurrence(n - 1)
                mix(n, lambda: recurrence_root(n - 1))
            recurrence(NB - 1)

            def gate(n, after_g):
                act.wait_ge(unit_done, U_GATE + 4 * n + 1)
                wait(act, yb_lo_ready, n)
                A(gel[:, :], ps[:, 0, :], ACT.Gelu_apprx_tanh).then_inc(gelu_ready, 1)
                split_hi(U_GATE + 4 * n + 4, 0)
                after_g()
                act.wait_ge(unit_done, U_GATE + 4 * n + 2)
                wait(act, m_part, n)
                A(sig_a[:, :], ps[:, 1, :], ACT.Sigmoid).then_inc(siga_ready, 1)
                split_hi(U_GATE + 4 * n + 5, 1)
                act.wait_ge(yb_f32, n + 1)
                A(yb_hi[:, ds(n, 1), :], gel[:, None, :], ACT.Copy).then_inc(yb_hi_ready, 1)
                split_hi(U_GATE + 4 * n + 6, 2)
                act.wait_ge(unit_done, U_GATE + 4 * n + 4)
                A(sig_b[:, ds(n, 1), :], ps[:, 3:4, :], ACT.Sigmoid).then_inc(sigb_ready, 1)
                split_hi(U_GATE + 4 * n + 7, 3)
                act.wait_ge(mod_sum, n + 1)
                A(modb[:, ds(n * HALF, HALF)], ps[:, B_T0, :], ACT.Copy).then_inc(mod_copied, 1)

            recurrence_root(NB - 1)
            act.wait_ge(scan_ready, NB)
            gate(0, lambda: None)
            with act.Fori(1, NB) as n:
                gate(n, lambda: None)

            with act.Fori(0, NB // RING) as q:
                for j in range(RING):
                    n = RING * q + j
                    act.wait_ge(m_f32, n + 1)
                    A(m_hi[:, ds(n, 1), :], hm[:, ds(n, 1), :], ACT.Copy).then_inc(m_hi_ready, 1)
                    split_hi(U_BOUT + n + RING, j)
            for j in range(RING):
                act.wait_ge(raw_in[j], 16 * ((U_WO + RING + j) // RING + 1))
                A(wo2_hi[:, j, :], raw[:, j, :], ACT.Copy).then_inc(w_hi_ready, 1)

            for t in range(TB):
                pair = ps[:, 2 * (t % 2):2 * (t % 2) + 2, :]
                if t < TB - 1:
                    act.wait_ge(y_done, t + 1)
                else:
                    act.wait_ge(unit_done, U_UP)
                A(junk[:, :].rearrange("p (a n) -> p a n", a=2), pair, ACT.Square, accum_out=stat[:, 8 + t:9 + t]).then_inc(y_sq, 1)
                act.wait_ge(y_sq, t + 1)
                A(stat[:, 12:13], stat[:, 8 + t:9 + t], ACT.Sqrt, scale=1.0 / D, bias=eps_t[:, 0:1]).then_inc(y_sqrt, 1)
                act.wait_ge(x1_ready, t + 1)
                A(junk[:, :], xs[:, t, :], ACT.Square, accum_out=stat[:, t:t + 1]).then_inc(x1_sq, 1)
                act.wait_ge(x1_sq, t + 1)
                A(stat[:, 13:14], stat[:, t:t + 1], ACT.Sqrt, scale=1.0 / D, bias=eps_t[:, 0:1]).then_inc(x1_sqrt, 1)
                act.wait_ge(xn2_tr, t + 1)
                wait(act, h2_lo_ready, t)
                for k in range(NB):
                    A(h2f[:, k, :], ps[:, B_R + k // 4 + 2 * (t % 2), (k % 4) * P:(k % 4 + 1) * P], ACT.Identity,
                      scale=s_mlp[:, k:k + 1], bias=mcol[:, 2 * NB + k:2 * NB + k + 1]).then_inc(h2_f32, 1)
                act.wait_ge(h2_f32, NB * (t + 1))
                A(h2_hi[:, :, t * P:(t + 1) * P], h2f[:, :, :], ACT.Copy).then_inc(h2_hi_ready, 1)
            for j in range(RING):
                split_hi(U_UP + j, j, U_WO + j + 1)

            def up(n, j):
                act.wait_ge(unit_done, U_UP + n + 1)
                wait(act, hid_ready, n - 1)
                A(relu_t[:, j % 2, :], ps[:, j, :], ACT.Relu).then_inc(relu_ready, 1)
                split_hi(U_UP + n + RING, j)

            def hidden_hi(n, j):
                if not isinstance(n, int):
                    act.wait_ge(unit_done, U_DOWN + n - RING + 1)
                act.wait_ge(hid_ready, n + 1)
                A(hd_hi[:, ds(j, 1), :], hid[:, ds(n, 1), :], ACT.Copy).then_inc(hd_hi_ready, 1)

            for n in range(2):
                up(n, n)
            with act.Fori(0, FB // RING - 1) as q:
                for j in range(RING):
                    up(RING * q + j + 2, (j + 2) % RING)
            for j in range(RING):
                hidden_hi(j, j)
            for n in range(FB - 2, FB):
                up(n, n % RING)

            with act.Fori(0, FB // RING - 1) as q:
                for j in range(RING):
                    hidden_hi(RING * q + j + RING, j)
                    split_hi(U_DOWN + RING * q + j + RING, j)

            for t in range(TB):
                act.wait_ge(z_done, t + 1)
                A(junk2[:, :].rearrange("p (a n) -> p a n", a=2), ps[:, 2 * t:2 * t + 2, :], ACT.Square,
                  accum_out=stat[:, 8 + t:9 + t]).then_inc(z_sq, 1)
                act.wait_ge(z_sq, t + 1)
                A(stat[:, 12 + t:13 + t], stat[:, 8 + t:9 + t], ACT.Sqrt, scale=1.0 / D, bias=eps_t[:, 0:1]).then_inc(z_sqrt, 1)

        @block.vector
        def _(dve):
            V = nc.vector

            def f(t):
                return t.bitcast(f32)

            def split_lo(u, slot):
                dve.wait_ge(w_hi_ready, u + 1)
                V.tensor_tensor(w_lo[:, slot, :], raw[:, slot, :], f(w_hi[:, slot, :]), ALU.subtract).then_inc(w_lo_ready, 1)

            dve.wait_ge(cols_sum, 1)
            V.tensor_copy(cols[:, 0:NCOL], ps[:, B_T0, 0:NCOL]).then_inc(cols_ready, 1)
            dve.wait_ge(cols_ready, 1)
            V.scalar_tensor_tensor(sp[:, 0, :], cols[:, C_LAM:C_LAM + NB], -1.0, cols[:, C_LAM:C_LAM + NB],
                                   ALU.mult, ALU.min).then_inc(sp_step, 1)
            dve.wait_ge(sig_c, 1)
            V.tensor_tensor(c_act[:, :], c_act[:, :], cols[:, C_C:C_C + NB], ALU.mult).then_inc(cact, 1)
            dve.wait_ge(bmod0_in, 16)
            dve.wait_ge(cact, 1)

            def mod0_step(k):
                dve.wait_ge(mod0_in[k % 2], 16 * (k // 2 + 1))
                wait(dve, mod0_acc, k)
                V.scalar_tensor_tensor(mod0[:, :], mod0_raw[:, k % 2, :], c_act[:, k:k + 1], mod0[:, :],
                                       ALU.mult, ALU.add).then_inc(mod0_acc, 1)

            for k in range(2):
                mod0_step(k)
            dve.wait_ge(x_sqrt, 1)
            V.reciprocal(stat[:, 8:12], stat[:, 4:8]).then_inc(x_rstd, 1)
            dve.wait_ge(x_rstd, 1)
            for t in range(TB):
                V.tensor_scalar(xs[:, t, :], xs[:, t, :], stat[:, 8 + t:9 + t], None, ALU.mult).then_inc(x_norm, 1)
            for k in range(2, NB):
                mod0_step(k)
            step = [1]

            def chain(ins):
                step[0] += 1
                ins.then_inc(sp_step, 1)
                dve.wait_ge(sp_step, step[0])

            dve.wait_ge(sp_act, 1)
            chain(V.tensor_scalar(sp[:, 2, :], sp[:, 1, :], 2.0, None, ALU.add))
            chain(V.reciprocal(sp[:, 3, :], sp[:, 2, :]))
            chain(V.tensor_tensor(sp[:, 2, :], sp[:, 1, :], sp[:, 3, :], ALU.mult))
            chain(V.tensor_tensor(sp[:, 3, :], sp[:, 2, :], sp[:, 2, :], ALU.mult))
            chain(V.tensor_scalar(sp[:, 4, :], sp[:, 3, :], 1.0 / 17, None, ALU.mult))
            for odd in (15, 13, 11, 9, 7, 5, 3):
                chain(V.scalar_tensor_tensor(sp[:, 4, :], sp[:, 4, :], 1.0 / odd, sp[:, 3, :], ALU.add, ALU.mult))
            chain(V.scalar_tensor_tensor(sp[:, 4, :], sp[:, 4, :], 1.0, sp[:, 2, :], ALU.add, ALU.mult))
            chain(V.tensor_scalar(sp[:, 5, :], cols[:, C_LAM:C_LAM + NB], -LRU_C, 0.0, ALU.mult, ALU.max))
            chain(V.scalar_tensor_tensor(k_pos[:, :], sp[:, 4, :], 2.0 * LRU_C, sp[:, 5, :], ALU.mult, ALU.add))
            V.tensor_scalar(k_neg[:, :], k_pos[:, :], -1.0, None, ALU.mult).then_inc(cols_ready, 1)

            def diagonal(dst, src, count):
                blocks = HALF // P
                tmp = dtmp[:, 0:HALF].rearrange("p (b j) -> p b j", b=blocks)
                V.tensor_tensor(tmp, src.rearrange("p (b j) -> p b j", b=blocks),
                                ident[:, None, :].to_broadcast([P, blocks, P]), ALU.mult).then_inc(diag_step, 1)
                dve.wait_ge(diag_step, 2 * count + 1)
                V.tensor_reduce(dst, tmp, AX.X, ALU.add).then_inc(diag_step, 1)
                dve.wait_ge(diag_step, 2 * count + 2)

            dve.wait_ge(x_sqrt, 1)
            for q in range(4):
                dve.wait_ge(mod0_sum, q + 1)
                diagonal(mcol[:, 4 * q:4 * q + 4], ps[:, 4 + q, :] if q < 2 else ps[:, 4 + q, :], q)
            V.scalar_tensor_tensor(s_mix[:, :], mcol[:, NB:2 * NB], 1.0, cols[:, C_GX:C_GX + NB],
                                   ALU.add, ALU.mult).then_inc(col0_ready, 1)
            dve.wait_ge(col0_ready, 1)
            for k in range(NB):
                dve.wait_ge(xnt_ready, k + 1)
                V.tensor_scalar(xnt[:, k, :], xnt[:, k, :], s_mix[:, k:k + 1], mcol[:, k:k + 1],
                                ALU.mult, ALU.add).then_inc(h_f32, 1)
                if k < RING:
                    split_lo(k, k)
                if k >= 1:
                    dve.wait_ge(h_hi, k)
                    V.tensor_tensor(ht_lo[:, k - 1, :], xnt[:, k - 1, :], f(ht_hi[:, k - 1, :]), ALU.subtract).then_inc(h_lo, 1)
            dve.wait_ge(h_hi, NB)
            V.tensor_tensor(ht_lo[:, NB - 1, :], xnt[:, NB - 1, :], f(ht_hi[:, NB - 1, :]), ALU.subtract).then_inc(h_lo, 1)

            def recurrence_gates(n):
                dve.wait_ge(i_ready, n + 1)
                V.tensor_tensor(i_t[:, :], i_t[:, :], xc[:, :], ALU.mult).then_inc(ix_ready, 1)
                dve.wait_ge(q_ready, n + 1)
                V.scalar_tensor_tensor(q_t[:, :], q_t[:, :], 1.0, t_t[:, :], ALU.add, ALU.mult).then_inc(q2_ready, 1)

            def recurrence_scan(n):
                dve.wait_ge(mult_ready, n + 1)
                dve.wait_ge(ix_ready, n + 1)
                V.tensor_tensor(i_t[:, :], i_t[:, :], q_t[:, :], ALU.mult).then_inc(bx_ready, 1)
                dve.wait_ge(bx_ready, n + 1)
                V.tensor_tensor_scan(hm[:, ds(n, 1), :].rearrange("p a n -> p (a n)"), a_t[:, :], i_t[:, :], 0.0, ALU.mult, ALU.add).then_inc(scan_ready, 1)

            def mix(n, after_conv):
                dve.wait_ge(xc_tap, n + 1)
                for k in range(KB - 1):
                    wait(dve, xc_conv, 3 * n + k)
                    V.scalar_tensor_tensor(xc[:, :], xbp[:, k:k + SEQ], cols[:, ds(C_BW + k * NB + n, 1)], xc[:, :],
                                           ALU.mult, ALU.add).then_inc(xc_conv, 1)
                split_lo(4 * n + 4, 0)
                after_conv()
                dve.wait_ge(xc_hi_ready, n + 1)
                wait(dve, gates_done, n)
                V.tensor_tensor(xc_lo[:, :], xc[:, :], f(xc_hi[:, :]), ALU.subtract).then_inc(xc_lo_ready, 1)
                dve.wait_ge(g_hi_ready, n + 1)
                V.tensor_tensor(g_lo[:, :, :], graw[:, :, :], f(g_hi[:, :, :]), ALU.subtract).then_inc(g_lo_ready, 1)
                split_lo(4 * n + 5, 1)
                dve.wait_ge(unit_done, 4 * n + 3)
                dve.wait_ge(c_copied, n + 1)
                wait(dve, ca_tap, n)
                V.tensor_tensor(cvp[:, KA - 1:], c_sb[:, :], ps[:, 2, :], ALU.mult).then_inc(cv_ready, 1)
                split_lo(4 * n + 6, 2)
                dve.wait_ge(ca_tap, n + 1)
                for k in range(KA - 1):
                    wait(dve, ca_conv, 2 * n + k)
                    V.scalar_tensor_tensor(ca[:, :], cvp[:, k:k + SEQ], cols[:, ds(C_AW + k * NB + n, 1)], ca[:, :],
                                           ALU.mult, ALU.add).then_inc(ca_conv, 1)
                dve.wait_ge(unit_done, 4 * n + 4)
                dve.wait_ge(ca_conv, 2 * (n + 1))
                V.tensor_tensor(ca[:, :], ca[:, :], ps[:, 3, :], ALU.mult).then_inc(ya_f32, 1)
                dve.wait_ge(ya_hi_ready, n + 1)
                V.tensor_tensor(ya_lo[:, ds(n, 1), :], ca[:, None, :], f(ya_hi[:, ds(n, 1), :]), ALU.subtract).then_inc(ya_lo_ready, 1)
                split_lo(4 * n + 7, 3)

            mix(0, lambda: None)
            with dve.Fori(1, NB) as n:
                recurrence_gates(n - 1)
                mix(n, lambda: recurrence_scan(n - 1))
            recurrence_gates(NB - 1)
            recurrence_scan(NB - 1)

            dve.wait_ge(bmod_in, 16)

            def gate(n):
                def mod_chunk(j):
                    dve.wait_ge(modraw_in[j % 2], 16 * (2 * n + j // 2 + 1))
                    for a in range(2):
                        wait(dve, mod_acc, 8 * n + 2 * j + a)
                        V.scalar_tensor_tensor(modb[:, ds(n * HALF, HALF)], modraw[:, j % 2, a, :],
                                               c_act[:, 2 * j + a:2 * j + a + 1], modb[:, ds(n * HALF, HALF)],
                                               ALU.mult, ALU.add).then_inc(mod_acc, 1)

                mod_chunk(0)
                dve.wait_ge(gelu_ready, n + 1)
                dve.wait_ge(scan_ready, n + 1)
                V.tensor_tensor(gel[:, None, :], gel[:, None, :], hm[:, ds(n, 1), :], ALU.mult).then_inc(yb_f32, 1)
                split_lo(U_GATE + 4 * n + 4, 0)
                mod_chunk(1)
                split_lo(U_GATE + 4 * n + 5, 1)
                dve.wait_ge(yb_hi_ready, n + 1)
                V.tensor_tensor(yb_lo[:, ds(n, 1), :], gel[:, None, :], f(yb_hi[:, ds(n, 1), :]), ALU.subtract).then_inc(yb_lo_ready, 1)
                mod_chunk(2)
                dve.wait_ge(unit_done, U_GATE + 4 * n + 3)
                dve.wait_ge(siga_ready, n + 1)
                V.tensor_tensor(hm[:, ds(n, 1), :], sig_a[:, None, :], ps[:, 2:3, :], ALU.mult).then_inc(m_part, 1)
                split_lo(U_GATE + 4 * n + 6, 2)
                mod_chunk(3)
                split_lo(U_GATE + 4 * n + 7, 3)

            gate(0)
            with dve.Fori(1, NB) as n:
                gate(n)

            with dve.Fori(0, NB // RING) as q:
                for j in range(RING):
                    n = RING * q + j
                    dve.wait_ge(unit_done, U_BOUT + n + 1)
                    dve.wait_ge(sigb_ready, n + 1)
                    V.tensor_tensor(sig_b[:, ds(n, 1), :], sig_b[:, ds(n, 1), :], ps[:, j:j + 1, :], ALU.mult).then_inc(bout_scaled, 1)
                    dve.wait_ge(bout_scaled, n + 1)
                    V.tensor_tensor(hm[:, ds(n, 1), :], hm[:, ds(n, 1), :], sig_b[:, ds(n, 1), :], ALU.add).then_inc(m_f32, 1)
                    dve.wait_ge(m_hi_ready, n + 1)
                    V.tensor_tensor(m_lo[:, ds(n, 1), :], hm[:, ds(n, 1), :], f(m_hi[:, ds(n, 1), :]), ALU.subtract).then_inc(m_lo_ready, 1)
                    split_lo(U_BOUT + n + RING, j)
            for j in range(RING):
                dve.wait_ge(w_hi_ready, U_WO + RING + j + 1)
                V.tensor_tensor(wo2_lo[:, j, :], raw[:, j, :], f(wo2_hi[:, j, :]), ALU.subtract).then_inc(w_lo_ready, 1)

            dve.wait_ge(gbc_in, 32)
            dve.wait_ge(mod_copied, 8)
            V.tensor_tensor(modb[:, 0:D], modb[:, 0:D], g_bc[:, 0, :], ALU.mult).then_inc(gm_ready, 1)
            V.tensor_tensor(modb[:, 3 * D:4 * D], modb[:, 3 * D:4 * D], g_bc[:, 1, :], ALU.mult).then_inc(gm_ready, 1)
            for q in range(4):
                diagonal(mcol[:, 2 * NB + 4 * q:2 * NB + 4 * q + 4], modb[:, D + q * HALF:D + (q + 1) * HALF], 4 + q)
            V.scalar_tensor_tensor(s_mlp[:, :], mcol[:, 3 * NB:4 * NB], 1.0, cols[:, C_GM:C_GM + NB],
                                   ALU.add, ALU.mult).then_inc(colf_ready, 1)

            dve.wait_ge(gm_ready, 2)
            dve.wait_ge(m_lo_ready, NB)
            for t in range(TB):
                dve.wait_ge(y_sqrt, t + 1)
                V.reciprocal(stat[:, 14:15], stat[:, 12:13]).then_inc(y_rstd, 1)
                dve.wait_ge(y_rstd, t + 1)
                for h in range(2):
                    V.scalar_tensor_tensor(y1[:, h * HALF:(h + 1) * HALF], ps[:, 2 * (t % 2) + h, :], stat[:, 14:15],
                                           modb[:, h * HALF:(h + 1) * HALF], ALU.mult, ALU.mult).then_inc(y_scaled, 1)
                dve.wait_ge(y_scaled, 2 * t + 2)
                dve.wait_ge(xr_in[t], 32)
                V.tensor_tensor(xs[:, t, :], xs[:, t, :], y1[:, :], ALU.add).then_inc(x1_ready, 1)
                dve.wait_ge(x1_sqrt, t + 1)
                V.reciprocal(stat[:, 15:16], stat[:, 13:14]).then_inc(x1_rstd, 1)
                dve.wait_ge(x1_rstd, t + 1)
                wait(dve, xn2_tr, t)
                V.tensor_scalar(xn2[:, :], xs[:, t, :], stat[:, 15:16], None, ALU.mult).then_inc(xn2_ready, 1)
                dve.wait_ge(h2_hi_ready, t + 1)
                V.tensor_tensor(h2_lo[:, :, t * P:(t + 1) * P], h2f[:, :, :], f(h2_hi[:, :, t * P:(t + 1) * P]),
                                ALU.subtract).then_inc(h2_lo_ready, 1)
            for j in range(RING):
                split_lo(U_UP + j, j)

            def up(n, j):
                dve.wait_ge(relu_ready, n + 1)
                r = relu_t[:, j % 2:j % 2 + 1, :]
                V.tensor_tensor(hid[:, ds(n, 1), :], r, r, ALU.mult).then_inc(hid_ready, 1)
                split_lo(U_UP + n + RING, j)

            def hidden_lo(n, j):
                dve.wait_ge(hd_hi_ready, n + 1)
                V.tensor_tensor(hd_lo[:, ds(j, 1), :], hid[:, ds(n, 1), :], f(hd_hi[:, ds(j, 1), :]),
                                ALU.subtract).then_inc(hd_lo_ready, 1)

            for n in range(2):
                up(n, n)
            with dve.Fori(0, FB // RING - 1) as q:
                for j in range(RING):
                    up(RING * q + j + 2, (j + 2) % RING)
            for j in range(RING):
                hidden_lo(j, j)
            for n in range(FB - 2, FB):
                up(n, n % RING)
            with dve.Fori(0, FB // RING - 1) as q:
                for j in range(RING):
                    hidden_lo(RING * q + j + RING, j)
                    split_lo(U_DOWN + RING * q + j + RING, j)
            for t in range(TB):
                dve.wait_ge(z_sqrt, t + 1)
                V.reciprocal(stat[:, t:t + 1], stat[:, 12 + t:13 + t]).then_inc(z_rstd, 1)
                dve.wait_ge(z_rstd, t + 1)
                for h in range(2):
                    V.scalar_tensor_tensor(y2[:, h * HALF:(h + 1) * HALF], ps[:, 2 * t + h, :], stat[:, t:t + 1],
                                           modb[:, 3 * D + h * HALF:3 * D + (h + 1) * HALF], ALU.mult, ALU.mult).then_inc(z_scaled, 1)
                for h in range(2):
                    dve.wait_ge(z_scaled, 2 * t + h + 1)
                    V.tensor_tensor(xs[:, t, h * HALF:(h + 1) * HALF], xs[:, t, h * HALF:(h + 1) * HALF],
                                    y2[:, h * HALF:(h + 1) * HALF], ALU.add).then_inc(z_out, 1)

        @block.tensor
        def _(pe):
            def column_unit(u, slot, r_hi, r_lo, bank):
                pe.wait_ge(w_lo_ready, u + 1)
                for k in range(NB):
                    last = mm3(ps[:, bank, :], w_hi[:, slot, k * P:(k + 1) * P], w_lo[:, slot, k * P:(k + 1) * P],
                               r_hi[:, k, :], r_lo[:, k, :], k == 0, k == NB - 1)
                last.then_inc(unit_done, 1)

            pe.wait_ge(vec_in, 16 * (len(vectors) + 2))
            pe.wait_ge(const_ready, 4)
            nc.tensor.transpose(ps[:, B_T0, 0:NCOL], vrows[0:NCOL, :], ident[0:NCOL, 0:NCOL]).then_inc(cols_sum, 1)
            pe.wait_ge(cols_ready, 1)
            pe.wait_ge(x_norm, TB)
            for k in range(NB):
                for t in range(TB):
                    last = nc.tensor.transpose(ps[:, k, t * P:(t + 1) * P], xs[:, t, k * P:(k + 1) * P], ident[:, :])
                last.then_inc(x_tr, 1)
            pe.wait_ge(mod0_acc, NB)
            for q in range(4):
                pe.wait_ge(xnt_ready, 4 + q + 1)
                nc.tensor.matmul(ps[:, 4 + q, :], ones[:, :], mod0[:, q * HALF:(q + 1) * HALF],
                                 start=True, stop=True).then_inc(mod0_sum, 1)
            pe.wait_ge(h_lo, NB)

            def mix(n):
                wait(pe, xc_tap, n)
                column_unit(4 * n, 0, ht_hi, ht_lo, 0)
                wait(pe, c_copied, n)
                column_unit(4 * n + 1, 1, ht_hi, ht_lo, 1)
                wait(pe, cv_ready, n)
                column_unit(4 * n + 2, 2, ht_hi, ht_lo, 2)
                wait(pe, ya_f32, n)
                column_unit(4 * n + 3, 3, ht_hi, ht_lo, 3)
                pe.wait_ge(xc_lo_ready, n + 1)
                pe.wait_ge(g_lo_ready, n + 1)
                wait(pe, r_ready, n)
                mm3(ps[:, B_R, :], g_hi[:, 0, :], g_lo[:, 0, :], xc_hi[:, :], xc_lo[:, :], True, True)
                wait(pe, i_ready, n)
                mm3(ps[:, B_I, :], g_hi[:, 1, :], g_lo[:, 1, :], xc_hi[:, :], xc_lo[:, :], True, True).then_inc(gates_done, 1)

            mix(0)
            with pe.Fori(1, NB) as n:
                mix(n)

            def gate(n, bank_sems, before):
                u = U_GATE + 4 * n
                pe.wait_ge(bank_sems[0], n + before)
                column_unit(u, 0, ht_hi, ht_lo, 0)
                pe.wait_ge(bank_sems[1], n + before)
                column_unit(u + 1, 1, ht_hi, ht_lo, 1)
                pe.wait_ge(bank_sems[2], n + before)
                pe.wait_ge(ya_lo_ready, NB)
                column_unit(u + 2, 2, ya_hi, ya_lo, 2)
                pe.wait_ge(bank_sems[3], n + before)
                column_unit(u + 3, 3, ht_hi, ht_lo, 3)
                pe.wait_ge(mod_acc, 8 * (n + 1))
                wait(pe, mod_copied, n)
                nc.tensor.matmul(ps[:, B_T0, :], ones[:, :], modb[:, ds(n * HALF, HALF)], start=True, stop=True).then_inc(mod_sum, 1)

            gate(0, (xc_tap, c_copied, cv_ready, ya_f32), NB)
            with pe.Fori(1, NB) as n:
                gate(n, (gelu_ready, siga_ready, m_part, sigb_ready), 0)

            pe.wait_ge(yb_lo_ready, NB)
            for bank_sem in (gelu_ready, siga_ready, m_part, sigb_ready):
                pe.wait_ge(bank_sem, NB)
            for j in range(RING):
                column_unit(U_BOUT + j, j, yb_hi, yb_lo, j)
            with pe.Fori(1, NB // RING) as q:
                for j in range(RING):
                    pe.wait_ge(bout_scaled, RING * (q - 1) + j + 1)
                    column_unit(U_BOUT + RING * q + j, j, yb_hi, yb_lo, j)

            def transposes(t):
                pe.wait_ge(xn2_ready, t + 1)
                if t >= 2:
                    pe.wait_ge(h2_f32, NB * (t - 1))
                for k in range(NB):
                    last = nc.tensor.transpose(ps[:, B_R + k // 4 + 2 * (t % 2), (k % 4) * P:(k % 4 + 1) * P],
                                               xn2[:, k * P:(k + 1) * P], ident[:, :])
                last.then_inc(xn2_tr, 1)

            pe.wait_ge(bout_scaled, NB)
            pe.wait_ge(m_lo_ready, NB)
            for t in range(TB):
                if t >= 2:
                    pe.wait_ge(y_scaled, 2 * (t - 1))
                for k in range(NB):
                    if t == 0:
                        pe.wait_ge(w_lo_ready, U_WO + k + 1)
                    wh, wl = (w_hi, w_lo) if k < RING else (wo2_hi, wo2_lo)
                    for h in range(2):
                        cs = slice(h * HALF, (h + 1) * HALF)
                        last = mm3(ps[:, 2 * (t % 2) + h, :], m_hi[:, k, t * P:(t + 1) * P], m_lo[:, k, t * P:(t + 1) * P],
                                   wh[:, k % RING, cs], wl[:, k % RING, cs], k == 0, k == NB - 1)
                    if t == TB - 1:
                        last.then_inc(unit_done, 1)
                if t < TB - 1:
                    last.then_inc(y_done, 1)
                if t >= 1:
                    transposes(t - 1)
            transposes(TB - 1)

            pe.wait_ge(y_scaled, 2 * TB)
            pe.wait_ge(h2_lo_ready, TB)

            for j in range(RING):
                column_unit(U_UP + j, j, h2_hi, h2_lo, j)
            with pe.Fori(1, FB // RING) as q:
                for j in range(RING):
                    pe.wait_ge(relu_ready, RING * (q - 1) + j + 1)
                    column_unit(U_UP + RING * q + j, j, h2_hi, h2_lo, j)

            def down(slot, t, first, last):
                for h in range(2):
                    cs = slice(h * HALF, (h + 1) * HALF)
                    mm = mm3(ps[:, 2 * t + h, :], hd_hi[:, slot, t * P:(t + 1) * P], hd_lo[:, slot, t * P:(t + 1) * P],
                             w_hi[:, slot, cs], w_lo[:, slot, cs], first, last)
                return mm

            def split_ready(n):
                pe.wait_ge(hd_lo_ready, n + 1)
                pe.wait_ge(w_lo_ready, U_DOWN + n + 1)

            split_ready(0)
            for t in (2, 3, 0, 1):
                if t == 0:
                    pe.wait_ge(relu_ready, FB)
                mm = down(0, t, True, False)
            mm.then_inc(unit_done, 1)
            for n in range(1, RING):
                split_ready(n)
                for t in range(TB):
                    mm = down(n, t, False, False)
                mm.then_inc(unit_done, 1)
            with pe.Fori(1, FB // RING - 1) as q:
                for j in range(RING):
                    split_ready(RING * q + j)
                    for t in range(TB):
                        mm = down(j, t, False, False)
                    mm.then_inc(unit_done, 1)
            split_ready(FB - 1)
            for t in range(TB):
                for j in range(RING):
                    mm = down(j, t, False, j == RING - 1)
                mm.then_inc(z_done, 1)


_INS = ['x', 'c', 'w_mod', 'b_mod', 'g_pre_mix', 'g_post_mix', 'w_in', 'conv_a_w', 'conv_a_b',
        'w_a_out', 'conv_b_w', 'conv_b_b', 'w_gate_r', 'b_gate_r', 'w_gate_i', 'b_gate_i',
        'lru_lambda', 'w_b_out', 'w_o', 'g_pre_mlp', 'g_post_mlp', 'w_mlp_up', 'w_mlp_down']
_OUTS = [((1, 512, 1024), 'float32')]


def kernel(**inputs):
    import numpy as _np
    import concourse.bacc as _bacc
    from concourse import mybir as _mybir
    from concourse.bass_utils import run_bass_kernel_spmd as _run

    nc = _bacc.Bacc("TRN2", target_bir_lowering=False, num_devices=1)
    arrays, args = {}, []
    for name in _INS:
        a = _np.ascontiguousarray(inputs[name])
        arrays[f"in_{name}_dram"] = a
        args.append(nc.dram_tensor(f"in_{name}_dram", a.shape, _mybir.dt.from_np(a.dtype), kind="ExternalInput").ap())
    for i, (shape, dtype) in enumerate(_OUTS):
        dt = _mybir.dt.from_np(_np.dtype(dtype))
        args.append(nc.dram_tensor(f"out_{i}_dram", shape, dt, kind="ExternalOutput").ap())
    hybrid_layer_kernel(nc, *args)
    r = _run(nc, [arrays], core_ids=[0])
    return r.results[0]["out_0_dram"]
```

```python
import concourse.bass as bass
from concourse import mybir
from contextlib import ExitStack


def hybrid_layer_kernel(nc, x, c, w_mod, b_mod, g_pre_mix, g_post_mix, w_in, conv_a_w, conv_a_b,
                        w_a_out, conv_b_w, conv_b_b, w_gate_r, b_gate_r, w_gate_i, b_gate_i,
                        lru_lambda, w_b_out, w_o, g_pre_mlp, g_post_mlp, w_mlp_up, w_mlp_down, out):
    f32 = mybir.dt.float32
    f32r = mybir.dt.float32r
    ALU = mybir.AluOpType
    ACT = mybir.ActivationFunctionType
    AX = mybir.AxisListType
    ds = bass.ds

    P = 128
    SEQ, D = x.shape[1], x.shape[2]
    NB = D // P
    TB = SEQ // P
    FB = w_mlp_up.shape[2] // P
    HALF = D // 2
    KA, KB = conv_a_w.shape[1], conv_b_w.shape[1]
    EPS = 1e-6
    LRU_C = 8.0
    RING = 4
    U_MIX, U_GATE, U_BOUT, U_WO, U_UP = 0, 4 * NB, 8 * NB, 9 * NB, 10 * NB
    U_DOWN = U_UP + FB
    U_END = U_DOWN + FB

    w_in_v = w_in[0].rearrange("(k p) n -> p k n", p=P)
    w_a_v = w_a_out[0].rearrange("(k p) n -> p k n", p=P)
    w_b_v = w_b_out[0].rearrange("(k p) n -> p k n", p=P)
    w_o_v = w_o[0].rearrange("(k p) n -> p k n", p=P)
    w_up_v = w_mlp_up[0].rearrange("(k p) n -> p k n", p=P)
    w_dn_v = w_mlp_down[0].rearrange("(k p) n -> p k n", p=P)
    w_mod_v = w_mod[0].rearrange("(k p) n -> p k n", p=P)
    x_v = x[0].rearrange("(t p) d -> p t d", p=P)
    out_v = out[0].rearrange("(t p) d -> p t d", p=P)
    COL_B, COL_C, COL_V, COL_XB, COL_G, COL_UA, COL_UB = [j * D for j in range(7)]

    ctx = ExitStack()
    with ctx:
        def sem(name):
            return ctx.enter_context(nc.semaphore(name))

        def sb(name, shape, dt=f32):
            return ctx.enter_context(nc.sbuf_tensor(name, shape, dt))

        ident = sb("ident", [P, P])
        ones = sb("ones", [P, P])
        cols = sb("cols", [P, P])
        s_mix = sb("s_mix", [P, NB])
        s_mlp = sb("s_mlp", [P, NB])
        mcol = sb("mcol", [P, 4 * NB])
        c_act = sb("c_act", [P, NB])
        k_neg = sb("k_neg", [P, NB])
        k_pos = sb("k_pos", [P, NB])
        sp = sb("sp", [P, 6, NB])
        stat = sb("stat", [P, 16])
        eps_t = sb("eps_t", [P, 1])
        ysum = sb("ysum", [P, 3 * TB])
        zsum = sb("zsum", [P, 3 * TB])

        KIB = 1024
        ROW = SEQ * 4
        base = (nc.sbuf_base + 31) // 32 * 32
        room = nc.sbuf_usable_end - base - 512
        arena_bytes = 204 * KIB
        assert arena_bytes <= room, (arena_bytes, room)
        arena = ctx.enter_context(nc.sbuf_tensor("arena", [P, arena_bytes // 4], f32))
        O_XS, O_HT, O_YA, O_YB, O_RING, O_RAW, O_HM, O_MB, O_MR, O_GS = [
            base + KIB * k for k in (0, 16, 48, 80, 112, 144, 160, 176, 192, 200)]

        def at(name, shape, off, dt=f32):
            return nc.alloc_sbuf_tensor_at(name, shape, dt, offset=off)

        xs = at("xs", [P, TB, D], O_XS)
        sig_b = at("sig_b", [P, NB, SEQ], O_XS)
        ht_hi = at("ht_hi", [P, NB, SEQ], O_HT, f32r)
        ht_lo = at("ht_lo", [P, NB, SEQ], O_HT + 16 * KIB, f32r)
        wo2_hi = at("wo2_hi", [P, RING, D], O_HT, f32r)
        wo2_lo = at("wo2_lo", [P, RING, D], O_HT + 16 * KIB, f32r)
        ya_hi = at("ya_hi", [P, NB, SEQ], O_YA, f32r)
        ya_lo = at("ya_lo", [P, NB, SEQ], O_YA + 16 * KIB, f32r)
        m_hi = at("m_hi", [P, NB, SEQ], O_YA, f32r)
        m_lo = at("m_lo", [P, NB, SEQ], O_YA + 16 * KIB, f32r)
        hid = at("hid", [P, FB, SEQ], O_HT)
        yb_hi = at("yb_hi", [P, NB, SEQ], O_YB, f32r)
        yb_lo = at("yb_lo", [P, NB, SEQ], O_YB + 16 * KIB, f32r)
        h2_hi = at("h2_hi", [P, NB, SEQ], O_YB, f32r)
        h2_lo = at("h2_lo", [P, NB, SEQ], O_YB + 16 * KIB, f32r)
        w_hi = at("w_hi", [P, RING, D], O_RING, f32r)
        w_lo = at("w_lo", [P, RING, D], O_RING + 16 * KIB, f32r)
        raw = at("raw", [P, RING, D], O_RAW)
        xnt = at("xnt", [P, NB, SEQ], O_HM)
        hm = at("hm", [P, NB, SEQ], O_HM)
        modb = at("modb", [P, 4 * D], O_MB)
        modraw = at("modraw", [P, 2, 2, HALF], O_MR)
        g_bc = at("g_bc", [P, 2, D], O_MR)
        gel = at("gel", [P, SEQ], O_GS)
        sig_a = at("sig_a", [P, SEQ], O_GS + ROW)
        dtmp = at("dtmp", [P, D], O_GS)
        M0_BUFS = 3
        mod0_raw = at("mod0_raw", [P, M0_BUFS, NB, 2, P], O_YB)
        mod0 = at("mod0", [P, 2, D], O_YB + 24 * KIB)
        vrows = at("vrows", [P, P], O_MB)
        crows = at("crows", [NB, P], O_MB + KIB)
        raw0 = at("raw0", [P, RING, D], O_YA)
        w0_hi = at("w0_hi", [P, RING, D], O_XS, f32r)
        w0_lo = at("w0_lo", [P, RING, D], O_MB, f32r)
        xc, xc_hi, xc_lo, c_sb, ca, r_t, i_t, t_t, a_t, q_t = [
            at(nm, [P, SEQ], O_YB + ROW * k, f32r if nm in ("xc_hi", "xc_lo") else f32)
            for k, nm in enumerate("xc xc_hi xc_lo c_sb ca r_t i_t t_t a_t q_t".split())]
        g_hi = at("g_hi", [P, 2, P], O_YB + 20 * KIB, f32r)
        g_lo = at("g_lo", [P, 2, P], O_YB + 21 * KIB, f32r)
        graw = at("graw", [P, 2, P], O_YB + 22 * KIB)
        xbp = at("xbp", [P, KB - 1 + SEQ], O_YB + 25 * KIB)
        cvp = at("cvp", [P, KA - 1 + SEQ], O_YB + 28 * KIB)
        y1 = at("y1", [P, D], O_HM)
        xn2 = at("xn2", [P, D], O_HM + 4 * KIB)
        h2f = at("h2f", [P, NB, P], O_HM + 8 * KIB)
        junk = at("junk", [P, D], O_HM + 12 * KIB)
        junk0 = at("junk0", [P, D], O_GS)
        relu_t = at("relu_t", [P, 2, SEQ], O_GS)
        hd_hi = at("hd_hi", [P, RING, SEQ], O_HM, f32r)
        hd_lo = at("hd_lo", [P, RING, SEQ], O_HM + 8 * KIB, f32r)
        y2 = at("y2", [P, D], O_MR)
        junk2 = at("junk2", [P, D], O_GS)

        ps = ctx.enter_context(nc.psum_tensor("ps", [P, 8, HALF], f32))
        B_R, B_I, B_T0, B_T1 = 4, 5, 6, 7

        C_GX, C_GM, C_AW, C_AB, C_BW = 0, NB, 2 * NB, (2 + KA) * NB, (3 + KA) * NB
        C_BB = C_BW + KB * NB
        C_BR, C_BI, C_LAM = C_BB + NB, C_BB + 2 * NB, C_BB + 3 * NB
        NCOL = C_LAM + NB
        vectors = [(C_GX, g_pre_mix[0]), (C_GM, g_pre_mlp[0]), (C_AB, conv_a_b[0]),
                   (C_BB, conv_b_b[0]), (C_BR, b_gate_r[0]), (C_BI, b_gate_i[0]), (C_LAM, lru_lambda[0])]

        c_in = sem("c_in")
        c_sum = sem("c_sum")
        raw0a_in = sem("raw0a_in")
        raw0b_in = sem("raw0b_in")
        mod0_in2 = sem("mod0_in2")
        w0_hi_ready = sem("w0_hi_ready")
        w0_lo_ready = sem("w0_lo_ready")
        y_gained = sem("y_gained")
        z_gained = sem("z_gained")
        raw_in0 = sem("raw_in0")
        raw_in1 = sem("raw_in1")
        raw_in2 = sem("raw_in2")
        raw_in3 = sem("raw_in3")
        graw_in = sem("graw_in")
        loads_begun = sem("loads_begun")
        vec_in = sem("vec_in")
        xr_in0 = sem("xr_in0")
        xr_in1 = sem("xr_in1")
        xr_in2 = sem("xr_in2")
        xr_in3 = sem("xr_in3")
        mod0_in0 = sem("mod0_in0")
        mod0_in1 = sem("mod0_in1")
        modraw_in0 = sem("modraw_in0")
        modraw_in1 = sem("modraw_in1")
        bmod0_in = sem("bmod0_in")
        bmod_in = sem("bmod_in")
        gbc_in = sem("gbc_in")
        out_done = sem("out_done")
        const_ready = sem("const_ready")
        zero0_ready = sem("zero0_ready")
        zeromb_ready = sem("zeromb_ready")
        cols_sum = sem("cols_sum")
        cols_ready = sem("cols_ready")
        cact = sem("cact")
        sig_c = sem("sig_c")
        sp_act = sem("sp_act")
        sp_step = sem("sp_step")
        mod0_acc = sem("mod0_acc")
        mod0_sum = sem("mod0_sum")
        diag_step = sem("diag_step")
        col0_ready = sem("col0_ready")
        h_f32 = sem("h_f32")
        h_hi = sem("h_hi")
        h_lo = sem("h_lo")
        x_sq = sem("x_sq")
        x_var = sem("x_var")
        x_sqrt = sem("x_sqrt")
        x_rstd = sem("x_rstd")
        x_norm = sem("x_norm")
        x_tr = sem("x_tr")
        xnt_ready = sem("xnt_ready")
        w_hi_ready = sem("w_hi_ready")
        w_lo_ready = sem("w_lo_ready")
        unit_done = sem("unit_done")
        gates_done = sem("gates_done")
        xb_copied = sem("xb_copied")
        xc_tap = sem("xc_tap")
        xc_conv = sem("xc_conv")
        xc_hi_ready = sem("xc_hi_ready")
        xc_lo_ready = sem("xc_lo_ready")
        c_copied = sem("c_copied")
        cv_ready = sem("cv_ready")
        ca_tap = sem("ca_tap")
        ca_conv = sem("ca_conv")
        ya_f32 = sem("ya_f32")
        ya_hi_ready = sem("ya_hi_ready")
        ya_lo_ready = sem("ya_lo_ready")
        g_hi_ready = sem("g_hi_ready")
        g_lo_ready = sem("g_lo_ready")
        r_ready = sem("r_ready")
        i_ready = sem("i_ready")
        t_ready = sem("t_ready")
        a_ready = sem("a_ready")
        q_ready = sem("q_ready")
        q2_ready = sem("q2_ready")
        mult_ready = sem("mult_ready")
        ix_ready = sem("ix_ready")
        bx_ready = sem("bx_ready")
        scan_ready = sem("scan_ready")
        gelu_ready = sem("gelu_ready")
        yb_f32 = sem("yb_f32")
        yb_hi_ready = sem("yb_hi_ready")
        yb_lo_ready = sem("yb_lo_ready")
        siga_ready = sem("siga_ready")
        m_part = sem("m_part")
        sigb_ready = sem("sigb_ready")
        mod_acc = sem("mod_acc")
        mod_sum = sem("mod_sum")
        mod_copied = sem("mod_copied")
        gm_ready = sem("gm_ready")
        colf_ready = sem("colf_ready")
        bout_scaled = sem("bout_scaled")
        m_f32 = sem("m_f32")
        m_hi_ready = sem("m_hi_ready")
        m_lo_ready = sem("m_lo_ready")
        y_done = sem("y_done")
        y_sq = sem("y_sq")
        y_var = sem("y_var")
        y_sqrt = sem("y_sqrt")
        y_rstd = sem("y_rstd")
        y_scaled = sem("y_scaled")
        x1_ready = sem("x1_ready")
        x1_sq = sem("x1_sq")
        x1_var = sem("x1_var")
        x1_sqrt = sem("x1_sqrt")
        x1_rstd = sem("x1_rstd")
        xn2_ready = sem("xn2_ready")
        xn2_tr = sem("xn2_tr")
        h2_f32 = sem("h2_f32")
        h2_hi_ready = sem("h2_hi_ready")
        h2_lo_ready = sem("h2_lo_ready")
        relu_ready = sem("relu_ready")
        hid_ready = sem("hid_ready")
        hd_hi_ready = sem("hd_hi_ready")
        hd_lo_ready = sem("hd_lo_ready")
        z_done = sem("z_done")
        z_sq = sem("z_sq")
        z_var = sem("z_var")
        z_sqrt = sem("z_sqrt")
        z_rstd = sem("z_rstd")
        z_scaled = sem("z_scaled")
        z_out = sem("z_out")
        raw_in = [raw_in0, raw_in1, raw_in2, raw_in3]
        xr_in = [xr_in0, xr_in1, xr_in2, xr_in3]
        mod0_in = [mod0_in0, mod0_in1, mod0_in2]
        modraw_in = [modraw_in0, modraw_in1]

        def split_count(u):
            return u - RING + 1

        def wait(eng, semaphore, count):
            if not isinstance(count, int) or count > 0:
                eng.wait_ge(semaphore, count)

        def mm3(dst, l_hi, l_lo, r_hi, r_lo, first, last):
            nc.tensor.matmul(dst, l_hi, r_hi, start=first, stop=False)
            nc.tensor.matmul(dst, l_hi, r_lo, start=False, stop=False)
            return nc.tensor.matmul(dst, l_lo, r_hi, start=False, stop=last)

        block = ctx.enter_context(nc.Block())

        @block.sync
        def _(sp_eng):
            def load_unit(u, slot, src):
                wait(sp_eng, w_lo_ready, split_count(u - RING))
                sp_eng.sem_inc(loads_begun, 1)
                dst = raw[:, slot, :]
                if len(src.shape) == 3:
                    dst = dst.rearrange("p (k n) -> p k n", k=NB)
                sp_eng.dma_start(dst, src).then_inc(raw_in[slot], 16)

            def load_gates(n):
                wait(sp_eng, g_lo_ready, n)
                sp_eng.dma_start(graw[:, 0, :], w_gate_r[0, ds(n, 1)].rearrange("a p j -> p (a j)")).then_inc(graw_in, 16)
                sp_eng.dma_start(graw[:, 1, :], w_gate_i[0, ds(n, 1)].rearrange("a p j -> p (a j)")).then_inc(graw_in, 16)

            def load_mod0(j):
                wait(sp_eng, mod0_acc, NB * (j - M0_BUFS + 1))
                for a in range(2):
                    sp_eng.dma_start(mod0_raw[:, j % M0_BUFS, :, a, :],
                                     w_mod_v[:, :, a * D + j * P:a * D + (j + 1) * P]).then_inc(mod0_in[j % M0_BUFS], 16)

            def load_first_units(half, semaphore):
                ks = slice(half * NB // 2, (half + 1) * NB // 2)
                for j, col in enumerate((COL_XB, COL_C, COL_V, COL_B)):
                    sp_eng.dma_start(raw0[:, j, :].rearrange("p (k n) -> p k n", k=NB)[:, ks, :],
                                     w_in_v[:, ks, col:col + P]).then_inc(semaphore, 16)

            load_mod0(0)
            for t in range(TB):
                sp_eng.dma_start(xs[:, t, :], x_v[:, t, :]).then_inc(xr_in[t], 16)
            load_mod0(1)
            load_first_units(0, raw0a_in)
            load_unit(RING, 0, w_in_v[:, :, COL_XB + P:COL_XB + 2 * P])
            load_mod0(2)
            load_mod0(3)
            load_first_units(1, raw0b_in)
            load_mod0(4)
            load_mod0(5)
            load_unit(RING + 1, 1, w_in_v[:, :, COL_C + P:COL_C + 2 * P])
            load_mod0(6)
            load_mod0(7)
            load_unit(RING + 2, 2, w_in_v[:, :, COL_V + P:COL_V + 2 * P])
            load_unit(RING + 3, 3, w_in_v[:, :, COL_B + P:COL_B + 2 * P])
            sp_eng.wait_ge(mod0_acc, NB * NB)
            load_gates(0)
            load_gates(1)

            with sp_eng.Fori(2, NB) as n:
                for j, col in enumerate((COL_XB, COL_C, COL_V, COL_B)):
                    load_unit(4 * n + j, j, w_in_v[:, :, ds(col + n * P, P)])
                load_gates(n)

            gate_cols = ((w_in_v, COL_G), (w_in_v, COL_UA), (w_a_v, 0), (w_in_v, COL_UB))
            b_cols = tuple((w_b_v, j * P) for j in range(RING))
            for j, (view, col) in enumerate(gate_cols):
                load_unit(U_GATE + j, j, view[:, :, ds(col, P)])

            def mod_and_next(n, nxt, nxt_cols):
                for j, (view, col) in enumerate(nxt_cols):
                    wait(sp_eng, mod_acc, 8 * n + 2 * j - 2)
                    sp_eng.sem_inc(loads_begun, 1)
                    sp_eng.dma_start(modraw[:, j % 2, :, :],
                                     w_mod_v[:, 2 * j:2 * j + 2, ds(2 * D + n * HALF, HALF)]).then_inc(modraw_in[j % 2], 16)
                    load_unit(U_GATE + 4 * n + 4 + j, j, view[:, :, ds(col + nxt * P, P)])

            mod_and_next(0, 1, gate_cols)
            with sp_eng.Fori(1, NB - 1) as n:
                mod_and_next(n, n + 1, gate_cols)
            mod_and_next(NB - 1, 0, b_cols)
            for j in range(RING):
                load_unit(U_BOUT + RING + j, j, w_b_v[:, :, (RING + j) * P:(RING + j + 1) * P])
            sp_eng.wait_ge(mod_acc, 8 * NB)
            sp_eng.dma_start(g_bc[:, 0, :], g_post_mix[0:1, :].to_broadcast([P, D])).then_inc(gbc_in, 16)
            sp_eng.dma_start(g_bc[:, 1, :], g_post_mlp[0:1, :].to_broadcast([P, D])).then_inc(gbc_in, 16)
            for k in range(NB):
                load_unit(U_WO + k, k % RING, w_o_v[:, k, :])
            sp_eng.wait_ge(m_f32, NB)
            for t in range(TB):
                sp_eng.dma_start(xs[:, t, :], x_v[:, t, :]).then_inc(xr_in[t], 16)

            with sp_eng.Fori(0, FB // RING) as q:
                for j in range(RING):
                    load_unit(U_UP + RING * q + j, j, w_up_v[:, :, ds((RING * q + j) * P, P)])
            with sp_eng.Fori(0, FB // RING) as q:
                for j in range(RING):
                    load_unit(U_DOWN + RING * q + j, j, w_dn_v[:, ds(RING * q + j, 1), :].rearrange("p a n -> p (a n)"))
            for t in range(TB):
                for h in range(2):
                    sp_eng.wait_ge(z_out, 2 * t + h + 1)
                    sp_eng.dma_start(out_v[:, t, h * HALF:(h + 1) * HALF],
                                     xs[:, t, h * HALF:(h + 1) * HALF]).then_inc(out_done, 16)
            sp_eng.wait_ge(out_done, 16 * 2 * TB)

        @block.gpsimd
        def _(pool):
            nc.gpsimd.memset(ident[:, :], 0.0).then_inc(const_ready, 1)
            pool.wait_ge(const_ready, 1)
            nc.gpsimd.affine_select(out=ident[:, :], in_=ident[:, :], compare_op=ALU.not_equal, fill=1.0,
                                    base=0, pattern=[[-1, P]], channel_multiplier=1).then_inc(const_ready, 1)
            nc.gpsimd.memset(mod0[:, :, :], 0.0).then_inc(zero0_ready, 1)
            pool.wait_ge(zero0_ready, 1)
            pool.dma_start(mod0[0:1, :, :], b_mod[0:1, 0:2 * D].rearrange("a (b n) -> a b n", b=2)).then_inc(bmod0_in, 16)
            nc.gpsimd.memset(ones[:, :], 1.0).then_inc(const_ready, 1)
            nc.gpsimd.memset(eps_t[:, :], EPS).then_inc(const_ready, 1)
            pool.wait_ge(mod0_sum, NB)
            nc.gpsimd.memset(xbp[:, 0:KB - 1], 0.0).then_inc(const_ready, 1)
            nc.gpsimd.memset(cvp[:, 0:KA - 1], 0.0).then_inc(const_ready, 1)
            pool.wait_ge(unit_done, RING)
            nc.gpsimd.memset(modb[:, :], 0.0).then_inc(zeromb_ready, 1)
            pool.wait_ge(zeromb_ready, 1)
            pool.dma_start(modb[0:1, :], b_mod[0:1, 2 * D:6 * D]).then_inc(bmod_in, 16)

        @block.scalar
        def _(act):
            A = nc.scalar.activation

            def split_hi(u, slot, u_free=None):
                if u_free is None:
                    u_free = 0 if isinstance(u, int) and u < 2 * RING else u - RING + 1
                wait(act, unit_done, u_free)
                act.wait_ge(raw_in[slot], 16 * (u // RING))
                A(w_hi[:, slot, :], raw[:, slot, :], ACT.Copy).then_inc(w_hi_ready, 1)

            act.dma_start(crows[:, :], c[0].rearrange("(b p) -> b p", p=P)).then_inc(c_in, 16)
            for off, vec in vectors:
                act.dma_start(vrows[off:off + NB, :], vec.rearrange("(b p) -> b p", p=P)).then_inc(vec_in, 16)
            act.dma_start(vrows[C_AW:C_AW + KA * NB, :], conv_a_w[0].rearrange("k (b p) -> (k b) p", p=P)).then_inc(vec_in, 16)
            act.dma_start(vrows[C_BW:C_BW + KB * NB, :], conv_b_w[0].rearrange("k (b p) -> (k b) p", p=P)).then_inc(vec_in, 16)

            act.wait_ge(c_sum, 1)
            A(c_act[:, :], ps[:, B_T0, 0:NB], ACT.Sigmoid).then_inc(sig_c, 1)
            for t in range(TB):
                act.wait_ge(xr_in[t], 16)
                wait(act, x_sq, t)
                A(junk0[:, :], xs[:, t, :], ACT.Square, accum_out=stat[:, t:t + 1]).then_inc(x_sq, 1)
            act.wait_ge(x_sq, TB)
            act.wait_ge(const_ready, 4)
            A(stat[:, 4:8], stat[:, 0:4], ACT.Sqrt, scale=1.0 / D, bias=eps_t[:, 0:1]).then_inc(x_sqrt, 1)

            def first_units_hi(q):
                cs = slice(2 * q * P, 2 * (q + 1) * P)
                A(w0_hi[:, :, cs], raw0[:, :, cs], ACT.Copy).then_inc(w0_hi_ready, 1)

            for k in range(NB):
                act.wait_ge(x_tr, k + 1)
                A(xnt[:, k, :], ps[:, k, :], ACT.Copy).then_inc(xnt_ready, 1)
            act.wait_ge(raw0a_in, 16 * RING)
            first_units_hi(0)
            split_hi(RING, 0)
            for k in range(NB):
                act.wait_ge(col0_ready, 2 * (k + 1))
                A(xnt[:, k, :], xnt[:, k, :], ACT.Identity, scale=s_mix[:, k:k + 1], bias=mcol[:, k:k + 1]).then_inc(h_f32, 1)
                act.wait_ge(h_f32, k + 1)
                A(ht_hi[:, k, :], xnt[:, k, :], ACT.Copy).then_inc(h_hi, 1)
                if k % 2 == 1 and k < NB - 1:
                    if k == 3:
                        act.wait_ge(raw0b_in, 16 * RING)
                    first_units_hi((k + 1) // 2)
            split_hi(RING + 1, 1)
            act.wait_ge(sp_step, 1)
            A(sp[:, 1, :], sp[:, 0, :], ACT.Exp).then_inc(sp_act, 1)

            def split_gates(n):
                wait(act, gates_done, n)
                act.wait_ge(graw_in, 32 * (n + 1))
                A(g_hi[:, :, :], graw[:, :, :], ACT.Copy).then_inc(g_hi_ready, 1)

            def recurrence(n):
                act.wait_ge(gates_done, n + 1)
                A(r_t[:, :], ps[:, B_R, :], ACT.Sigmoid, bias=cols[:, ds(C_BR + n, 1)]).then_inc(r_ready, 1)
                A(i_t[:, :], ps[:, B_I, :], ACT.Sigmoid, bias=cols[:, ds(C_BI + n, 1)]).then_inc(i_ready, 1)
                act.wait_ge(r_ready, n + 1)
                A(t_t[:, :], r_t[:, :], ACT.Tanh, scale=k_pos[:, ds(n, 1)]).then_inc(t_ready, 1)
                A(a_t[:, :], r_t[:, :], ACT.Exp, scale=k_neg[:, ds(n, 1)]).then_inc(a_ready, 1)
                act.wait_ge(a_ready, n + 1)
                A(q_t[:, :], a_t[:, :], ACT.Square).then_inc(q_ready, 1)

            def recurrence_root(n):
                act.wait_ge(q2_ready, n + 1)
                A(q_t[:, :], q_t[:, :], ACT.Sqrt).then_inc(mult_ready, 1)

            def mix(n, after_xb, splits, xb_bank=0):
                act.wait_ge(unit_done, 4 * n + 1)
                wait(act, xc_conv, 3 * n)
                A(xbp[:, KB - 1:], ps[:, xb_bank, :], ACT.Copy).then_inc(xb_copied, 1)
                wait(act, ix_ready, n)
                A(xc[:, :], ps[:, xb_bank, :], ACT.Identity, scale=cols[:, ds(C_BW + (KB - 1) * NB + n, 1)],
                  bias=cols[:, ds(C_BB + n, 1)]).then_inc(xc_tap, 1)
                if splits[0] is not None:
                    split_hi(splits[0], splits[0] % RING if isinstance(n, int) else 0)
                after_xb()
                wait(act, gates_done, n)
                act.wait_ge(xc_conv, 3 * (n + 1))
                A(xc_hi[:, :], xc[:, :], ACT.Copy).then_inc(xc_hi_ready, 1)
                split_gates(n)
                act.wait_ge(unit_done, 4 * n + 2)
                wait(act, cv_ready, n)
                A(c_sb[:, :], ps[:, 1, :], ACT.Copy).then_inc(c_copied, 1)
                if splits[1] is not None:
                    split_hi(splits[1], splits[1] % RING if isinstance(n, int) else 1)
                act.wait_ge(cv_ready, n + 1)
                wait(act, ya_lo_ready, n)
                A(ca[:, :], cvp[:, KA - 1:], ACT.Identity, scale=cols[:, ds(C_AW + (KA - 1) * NB + n, 1)],
                  bias=cols[:, ds(C_AB + n, 1)]).then_inc(ca_tap, 1)
                if splits[2] is not None:
                    split_hi(splits[2], splits[2] % RING if isinstance(n, int) else 2)
                act.wait_ge(ya_f32, n + 1)
                A(ya_hi[:, ds(n, 1), :], ca[:, None, :], ACT.Copy).then_inc(ya_hi_ready, 1)
                if splits[3] is not None:
                    split_hi(splits[3], splits[3] % RING if isinstance(n, int) else 3)

            act.wait_ge(const_ready, 6)
            act.wait_ge(cols_ready, 2)
            mix(0, lambda: None, (RING + 2, RING + 3, None, None))
            recurrence(0)
            mix(1, lambda: recurrence_root(0), tuple(2 * RING + j for j in range(RING)), B_T0)
            with act.Fori(2, NB) as n:
                recurrence(n - 1)
                mix(n, lambda: recurrence_root(n - 1), tuple(4 * n + RING + j for j in range(RING)))
            recurrence(NB - 1)

            def gate(n, after_g):
                act.wait_ge(unit_done, U_GATE + 4 * n + 1)
                wait(act, yb_lo_ready, n)
                A(gel[:, :], ps[:, 0, :], ACT.Gelu_apprx_tanh).then_inc(gelu_ready, 1)
                split_hi(U_GATE + 4 * n + 4, 0)
                after_g()
                act.wait_ge(unit_done, U_GATE + 4 * n + 2)
                wait(act, m_part, n)
                A(sig_a[:, :], ps[:, 1, :], ACT.Sigmoid).then_inc(siga_ready, 1)
                split_hi(U_GATE + 4 * n + 5, 1)
                act.wait_ge(yb_f32, n + 1)
                A(yb_hi[:, ds(n, 1), :], gel[:, None, :], ACT.Copy).then_inc(yb_hi_ready, 1)
                split_hi(U_GATE + 4 * n + 6, 2)
                act.wait_ge(unit_done, U_GATE + 4 * n + 4)
                A(sig_b[:, ds(n, 1), :], ps[:, 3:4, :], ACT.Sigmoid).then_inc(sigb_ready, 1)
                split_hi(U_GATE + 4 * n + 7, 3)
                act.wait_ge(mod_sum, n + 1)
                A(modb[:, ds(n * HALF, HALF)], ps[:, B_T0, :], ACT.Copy).then_inc(mod_copied, 1)

            recurrence_root(NB - 1)
            act.wait_ge(scan_ready, NB)
            gate(0, lambda: None)
            with act.Fori(1, NB) as n:
                gate(n, lambda: None)

            with act.Fori(0, NB // RING) as q:
                for j in range(RING):
                    n = RING * q + j
                    act.wait_ge(m_f32, n + 1)
                    A(m_hi[:, ds(n, 1), :], hm[:, ds(n, 1), :], ACT.Copy).then_inc(m_hi_ready, 1)
                    split_hi(U_BOUT + n + RING, j)
            for j in range(RING):
                act.wait_ge(raw_in[j], 16 * ((U_WO + RING + j) // RING))
                A(wo2_hi[:, j, :], raw[:, j, :], ACT.Copy).then_inc(w_hi_ready, 1)

            for t in range(TB):
                if t < TB - 1:
                    act.wait_ge(y_done, t + 1)
                else:
                    for j in range(RING):
                        split_hi(U_UP + j, j, U_WO + j + 1)
                    act.wait_ge(unit_done, U_UP)
                for h in range(2):
                    A(junk[:, h * HALF:(h + 1) * HALF], ps[:, 2 * (t % 2) + h, :], ACT.Square,
                      accum_out=ysum[:, 2 * t + h:2 * t + h + 1]).then_inc(y_sq, 1)
                act.wait_ge(y_sq, 3 * t + 1)
                A(ysum[:, 2 * TB + t:2 * TB + t + 1], ysum[:, 2 * t:2 * t + 1], ACT.Identity, scale=1.0 / D,
                  bias=eps_t[:, 0:1]).then_inc(y_sq, 1)
                act.wait_ge(y_sq, 3 * t + 3)
                A(stat[:, 12:13], ysum[:, 2 * t + 1:2 * t + 2], ACT.Sqrt, scale=1.0 / D,
                  bias=ysum[:, 2 * TB + t:2 * TB + t + 1]).then_inc(y_sqrt, 1)
                act.wait_ge(x1_ready, t + 1)
                A(junk[:, :], xs[:, t, :], ACT.Square, accum_out=stat[:, t:t + 1]).then_inc(x1_sq, 1)
                act.wait_ge(x1_sq, t + 1)
                A(stat[:, 13:14], stat[:, t:t + 1], ACT.Sqrt, scale=1.0 / D, bias=eps_t[:, 0:1]).then_inc(x1_sqrt, 1)
                act.wait_ge(xn2_tr, t + 1)
                wait(act, h2_lo_ready, t)
                for k in range(NB):
                    A(h2f[:, k, :], ps[:, B_R + k // 4 + 2 * (t % 2), (k % 4) * P:(k % 4 + 1) * P], ACT.Identity,
                      scale=s_mlp[:, k:k + 1], bias=mcol[:, 2 * NB + k:2 * NB + k + 1]).then_inc(h2_f32, 1)
                act.wait_ge(h2_f32, NB * (t + 1))
                A(h2_hi[:, :, t * P:(t + 1) * P], h2f[:, :, :], ACT.Copy).then_inc(h2_hi_ready, 1)

            def up(n, j):
                act.wait_ge(unit_done, U_UP + n + 1)
                wait(act, hid_ready, n - 1)
                A(relu_t[:, j % 2, :], ps[:, j, :], ACT.Relu).then_inc(relu_ready, 1)
                split_hi(U_UP + n + RING, j)

            def hidden_hi(n, j):
                if not isinstance(n, int):
                    act.wait_ge(unit_done, U_DOWN + n - RING + 1)
                act.wait_ge(hid_ready, n + 1)
                A(hd_hi[:, ds(j, 1), :], hid[:, ds(n, 1), :], ACT.Copy).then_inc(hd_hi_ready, 1)

            for n in range(2):
                up(n, n)
            with act.Fori(0, FB // RING - 1) as q:
                for j in range(RING):
                    up(RING * q + j + 2, (j + 2) % RING)
            for j in range(RING):
                hidden_hi(j, j)
            for n in range(FB - 2, FB):
                up(n, n % RING)

            with act.Fori(0, FB // RING - 1) as q:
                for j in range(RING):
                    hidden_hi(RING * q + j + RING, j)
                    split_hi(U_DOWN + RING * q + j + RING, j)

            for t in range(TB):
                for h in range(2):
                    act.wait_ge(z_done, 2 * t + h + 1)
                    A(junk2[:, h * HALF:(h + 1) * HALF], ps[:, 2 * t + h, :], ACT.Square,
                      accum_out=zsum[:, 2 * t + h:2 * t + h + 1]).then_inc(z_sq, 1)
                act.wait_ge(z_sq, 3 * t + 2)
                A(zsum[:, 2 * TB + t:2 * TB + t + 1], zsum[:, 2 * t:2 * t + 1], ACT.Identity, scale=1.0 / D,
                  bias=eps_t[:, 0:1]).then_inc(z_sq, 1)
                act.wait_ge(z_sq, 3 * t + 3)
                A(stat[:, 12 + t:13 + t], zsum[:, 2 * t + 1:2 * t + 2], ACT.Sqrt, scale=1.0 / D,
                  bias=zsum[:, 2 * TB + t:2 * TB + t + 1]).then_inc(z_sqrt, 1)

        @block.vector
        def _(dve):
            V = nc.vector

            def f(t):
                return t.bitcast(f32)

            def split_lo(u, slot):
                dve.wait_ge(w_hi_ready, split_count(u))
                V.tensor_tensor(w_lo[:, slot, :], raw[:, slot, :], f(w_hi[:, slot, :]), ALU.subtract).then_inc(w_lo_ready, 1)

            dve.wait_ge(sig_c, 1)
            V.tensor_tensor(c_act[:, :], c_act[:, :], ps[:, B_T0, 0:NB], ALU.mult).then_inc(cact, 1)
            dve.wait_ge(bmod0_in, 16)
            dve.wait_ge(cact, 1)

            def mod0_steps(j, ks):
                if ks.start == 0:
                    dve.wait_ge(mod0_in[j % M0_BUFS], 32 * (j // M0_BUFS + 1))
                acc = mod0[:, :, j * P:(j + 1) * P]
                for k in ks:
                    wait(dve, mod0_acc, NB * j + k)
                    V.scalar_tensor_tensor(acc, mod0_raw[:, j % M0_BUFS, k, :, :], c_act[:, k:k + 1], acc,
                                           ALU.mult, ALU.add).then_inc(mod0_acc, 1)

            mod0_steps(0, range(NB))
            dve.wait_ge(x_sqrt, 1)
            V.reciprocal(stat[:, 8:12], stat[:, 4:8]).then_inc(x_rstd, 1)
            dve.wait_ge(x_rstd, 1)
            for t in range(TB):
                V.tensor_scalar(xs[:, t, :], xs[:, t, :], stat[:, 8 + t:9 + t], None, ALU.mult).then_inc(x_norm, 1)
            dve.wait_ge(cols_sum, 1)
            V.tensor_copy(cols[:, 0:NCOL], ps[:, B_T1, 0:NCOL]).then_inc(cols_ready, 1)
            dve.wait_ge(cols_ready, 1)
            V.scalar_tensor_tensor(sp[:, 0, :], cols[:, C_LAM:C_LAM + NB], -1.0, cols[:, C_LAM:C_LAM + NB],
                                   ALU.mult, ALU.min).then_inc(sp_step, 1)
            for k in range(NB):
                if k + 1 < NB:
                    mod0_steps(k + 1, range(NB // 2))
                dve.wait_ge(mod0_sum, k + 1)
                V.tensor_copy(mcol[:, k:k + 1], ps[:, B_T1, 2 * k:2 * k + 1]).then_inc(col0_ready, 1)
                V.scalar_tensor_tensor(s_mix[:, k:k + 1], ps[:, B_T1, 2 * k + 1:2 * k + 2], 1.0, cols[:, C_GX + k:C_GX + k + 1],
                                       ALU.add, ALU.mult).then_inc(col0_ready, 1)
                if k + 1 < NB:
                    mod0_steps(k + 1, range(NB // 2, NB))
                if k % 2 == 0:
                    dve.wait_ge(w0_hi_ready, k // 2 + 1)
                    cs = slice(k * P, (k + 2) * P)
                    V.tensor_tensor(w0_lo[:, :, cs], raw0[:, :, cs], f(w0_hi[:, :, cs]), ALU.subtract).then_inc(w0_lo_ready, 1)
                if k == 0:
                    split_lo(RING, 0)
                dve.wait_ge(h_hi, k + 1)
                V.tensor_tensor(ht_lo[:, k, :], xnt[:, k, :], f(ht_hi[:, k, :]), ALU.subtract).then_inc(h_lo, 1)
            split_lo(RING + 1, 1)

            step = [1]

            def chain(ins):
                step[0] += 1
                ins.then_inc(sp_step, 1)
                dve.wait_ge(sp_step, step[0])

            dve.wait_ge(sp_act, 1)
            chain(V.tensor_scalar(sp[:, 2, :], sp[:, 1, :], 2.0, None, ALU.add))
            chain(V.reciprocal(sp[:, 3, :], sp[:, 2, :]))
            chain(V.tensor_tensor(sp[:, 2, :], sp[:, 1, :], sp[:, 3, :], ALU.mult))
            chain(V.tensor_tensor(sp[:, 3, :], sp[:, 2, :], sp[:, 2, :], ALU.mult))
            chain(V.tensor_scalar(sp[:, 4, :], sp[:, 3, :], 1.0 / 17, None, ALU.mult))
            for odd in (15, 13, 11, 9, 7, 5, 3):
                chain(V.scalar_tensor_tensor(sp[:, 4, :], sp[:, 4, :], 1.0 / odd, sp[:, 3, :], ALU.add, ALU.mult))
            chain(V.scalar_tensor_tensor(sp[:, 4, :], sp[:, 4, :], 1.0, sp[:, 2, :], ALU.add, ALU.mult))
            chain(V.tensor_scalar(sp[:, 5, :], cols[:, C_LAM:C_LAM + NB], -LRU_C, 0.0, ALU.mult, ALU.max))
            chain(V.scalar_tensor_tensor(k_pos[:, :], sp[:, 4, :], 2.0 * LRU_C, sp[:, 5, :], ALU.mult, ALU.add))
            V.tensor_scalar(k_neg[:, :], k_pos[:, :], -1.0, None, ALU.mult).then_inc(cols_ready, 1)

            def diagonal(dst, src, count):
                blocks = HALF // P
                tmp = dtmp[:, 0:HALF].rearrange("p (b j) -> p b j", b=blocks)
                V.tensor_tensor(tmp, src.rearrange("p (b j) -> p b j", b=blocks),
                                ident[:, None, :].to_broadcast([P, blocks, P]), ALU.mult).then_inc(diag_step, 1)
                dve.wait_ge(diag_step, 2 * count + 1)
                V.tensor_reduce(dst, tmp, AX.X, ALU.add).then_inc(diag_step, 1)
                dve.wait_ge(diag_step, 2 * count + 2)

            def recurrence_gates(n):
                dve.wait_ge(i_ready, n + 1)
                V.tensor_tensor(i_t[:, :], i_t[:, :], xc[:, :], ALU.mult).then_inc(ix_ready, 1)
                dve.wait_ge(q_ready, n + 1)
                V.scalar_tensor_tensor(q_t[:, :], q_t[:, :], 1.0, t_t[:, :], ALU.add, ALU.mult).then_inc(q2_ready, 1)

            def recurrence_scan(n):
                dve.wait_ge(mult_ready, n + 1)
                dve.wait_ge(ix_ready, n + 1)
                V.tensor_tensor(i_t[:, :], i_t[:, :], q_t[:, :], ALU.mult).then_inc(bx_ready, 1)
                dve.wait_ge(bx_ready, n + 1)
                V.tensor_tensor_scan(hm[:, ds(n, 1), :].rearrange("p a n -> p (a n)"), a_t[:, :], i_t[:, :], 0.0, ALU.mult, ALU.add).then_inc(scan_ready, 1)

            def mix(n, after_conv, splits):
                dve.wait_ge(xc_tap, n + 1)
                for k in range(KB - 1):
                    wait(dve, xc_conv, 3 * n + k)
                    V.scalar_tensor_tensor(xc[:, :], xbp[:, k:k + SEQ], cols[:, ds(C_BW + k * NB + n, 1)], xc[:, :],
                                           ALU.mult, ALU.add).then_inc(xc_conv, 1)
                if splits[0] is not None:
                    split_lo(splits[0], splits[0] % RING if isinstance(n, int) else 0)
                after_conv()
                dve.wait_ge(xc_hi_ready, n + 1)
                wait(dve, gates_done, n)
                V.tensor_tensor(xc_lo[:, :], xc[:, :], f(xc_hi[:, :]), ALU.subtract).then_inc(xc_lo_ready, 1)
                dve.wait_ge(g_hi_ready, n + 1)
                V.tensor_tensor(g_lo[:, :, :], graw[:, :, :], f(g_hi[:, :, :]), ALU.subtract).then_inc(g_lo_ready, 1)
                if splits[1] is not None:
                    split_lo(splits[1], splits[1] % RING if isinstance(n, int) else 1)
                dve.wait_ge(unit_done, 4 * n + 3)
                dve.wait_ge(c_copied, n + 1)
                wait(dve, ca_tap, n)
                V.tensor_tensor(cvp[:, KA - 1:], c_sb[:, :], ps[:, 2, :], ALU.mult).then_inc(cv_ready, 1)
                if splits[2] is not None:
                    split_lo(splits[2], splits[2] % RING if isinstance(n, int) else 2)
                dve.wait_ge(ca_tap, n + 1)
                for k in range(KA - 1):
                    wait(dve, ca_conv, 2 * n + k)
                    V.scalar_tensor_tensor(ca[:, :], cvp[:, k:k + SEQ], cols[:, ds(C_AW + k * NB + n, 1)], ca[:, :],
                                           ALU.mult, ALU.add).then_inc(ca_conv, 1)
                dve.wait_ge(unit_done, 4 * n + 4)
                dve.wait_ge(ca_conv, 2 * (n + 1))
                V.tensor_tensor(ca[:, :], ca[:, :], ps[:, 3, :], ALU.mult).then_inc(ya_f32, 1)
                dve.wait_ge(ya_hi_ready, n + 1)
                V.tensor_tensor(ya_lo[:, ds(n, 1), :], ca[:, None, :], f(ya_hi[:, ds(n, 1), :]), ALU.subtract).then_inc(ya_lo_ready, 1)
                if splits[3] is not None:
                    split_lo(splits[3], splits[3] % RING if isinstance(n, int) else 3)

            mix(0, lambda: None, (RING + 2, RING + 3, None, None))
            recurrence_gates(0)
            mix(1, lambda: recurrence_scan(0), tuple(2 * RING + j for j in range(RING)))
            with dve.Fori(2, NB) as n:
                recurrence_gates(n - 1)
                mix(n, lambda: recurrence_scan(n - 1), tuple(4 * n + RING + j for j in range(RING)))
            recurrence_gates(NB - 1)
            recurrence_scan(NB - 1)

            dve.wait_ge(bmod_in, 16)

            def gate(n):
                def mod_chunk(j):
                    dve.wait_ge(modraw_in[j % 2], 16 * (2 * n + j // 2 + 1))
                    for a in range(2):
                        wait(dve, mod_acc, 8 * n + 2 * j + a)
                        V.scalar_tensor_tensor(modb[:, ds(n * HALF, HALF)], modraw[:, j % 2, a, :],
                                               c_act[:, 2 * j + a:2 * j + a + 1], modb[:, ds(n * HALF, HALF)],
                                               ALU.mult, ALU.add).then_inc(mod_acc, 1)

                mod_chunk(0)
                dve.wait_ge(gelu_ready, n + 1)
                dve.wait_ge(scan_ready, n + 1)
                V.tensor_tensor(gel[:, None, :], gel[:, None, :], hm[:, ds(n, 1), :], ALU.mult).then_inc(yb_f32, 1)
                split_lo(U_GATE + 4 * n + 4, 0)
                mod_chunk(1)
                split_lo(U_GATE + 4 * n + 5, 1)
                dve.wait_ge(yb_hi_ready, n + 1)
                V.tensor_tensor(yb_lo[:, ds(n, 1), :], gel[:, None, :], f(yb_hi[:, ds(n, 1), :]), ALU.subtract).then_inc(yb_lo_ready, 1)
                mod_chunk(2)
                dve.wait_ge(unit_done, U_GATE + 4 * n + 3)
                dve.wait_ge(siga_ready, n + 1)
                V.tensor_tensor(hm[:, ds(n, 1), :], sig_a[:, None, :], ps[:, 2:3, :], ALU.mult).then_inc(m_part, 1)
                split_lo(U_GATE + 4 * n + 6, 2)
                mod_chunk(3)
                split_lo(U_GATE + 4 * n + 7, 3)

            gate(0)
            with dve.Fori(1, NB) as n:
                gate(n)

            with dve.Fori(0, NB // RING) as q:
                for j in range(RING):
                    n = RING * q + j
                    dve.wait_ge(unit_done, U_BOUT + n + 1)
                    dve.wait_ge(sigb_ready, n + 1)
                    V.tensor_tensor(sig_b[:, ds(n, 1), :], sig_b[:, ds(n, 1), :], ps[:, j:j + 1, :], ALU.mult).then_inc(bout_scaled, 1)
                    dve.wait_ge(bout_scaled, n + 1)
                    V.tensor_tensor(hm[:, ds(n, 1), :], hm[:, ds(n, 1), :], sig_b[:, ds(n, 1), :], ALU.add).then_inc(m_f32, 1)
                    dve.wait_ge(m_hi_ready, n + 1)
                    V.tensor_tensor(m_lo[:, ds(n, 1), :], hm[:, ds(n, 1), :], f(m_hi[:, ds(n, 1), :]), ALU.subtract).then_inc(m_lo_ready, 1)
                    split_lo(U_BOUT + n + RING, j)
            for j in range(RING):
                dve.wait_ge(w_hi_ready, split_count(U_WO + RING + j))
                V.tensor_tensor(wo2_lo[:, j, :], raw[:, j, :], f(wo2_hi[:, j, :]), ALU.subtract).then_inc(w_lo_ready, 1)

            dve.wait_ge(gbc_in, 32)
            dve.wait_ge(mod_copied, 8)
            V.tensor_tensor(modb[:, 0:D], modb[:, 0:D], g_bc[:, 0, :], ALU.mult).then_inc(gm_ready, 1)
            V.tensor_tensor(modb[:, 3 * D:4 * D], modb[:, 3 * D:4 * D], g_bc[:, 1, :], ALU.mult).then_inc(gm_ready, 1)
            for q in range(4):
                diagonal(mcol[:, 2 * NB + 4 * q:2 * NB + 4 * q + 4], modb[:, D + q * HALF:D + (q + 1) * HALF], q)
            V.scalar_tensor_tensor(s_mlp[:, :], mcol[:, 3 * NB:4 * NB], 1.0, cols[:, C_GM:C_GM + NB],
                                   ALU.add, ALU.mult).then_inc(colf_ready, 1)

            dve.wait_ge(gm_ready, 2)
            dve.wait_ge(m_lo_ready, NB)
            for t in range(TB):
                if t == TB - 1:
                    for j in range(RING):
                        split_lo(U_UP + j, j)
                for h in range(2):
                    dve.wait_ge(y_sq, 3 * t + h + 1)
                    V.tensor_tensor(y1[:, h * HALF:(h + 1) * HALF], ps[:, 2 * (t % 2) + h, :],
                                    modb[:, h * HALF:(h + 1) * HALF], ALU.mult).then_inc(y_gained, 1)
                dve.wait_ge(y_sqrt, t + 1)
                V.reciprocal(stat[:, 14:15], stat[:, 12:13]).then_inc(y_rstd, 1)
                dve.wait_ge(y_rstd, t + 1)
                dve.wait_ge(y_gained, 2 * t + 2)
                dve.wait_ge(xr_in[t], 32)
                V.scalar_tensor_tensor(xs[:, t, :], y1[:, :], stat[:, 14:15], xs[:, t, :], ALU.mult, ALU.add).then_inc(x1_ready, 1)
                dve.wait_ge(x1_sqrt, t + 1)
                V.reciprocal(stat[:, 15:16], stat[:, 13:14]).then_inc(x1_rstd, 1)
                dve.wait_ge(x1_rstd, t + 1)
                wait(dve, xn2_tr, t)
                V.tensor_scalar(xn2[:, :], xs[:, t, :], stat[:, 15:16], None, ALU.mult).then_inc(xn2_ready, 1)
                dve.wait_ge(h2_hi_ready, t + 1)
                V.tensor_tensor(h2_lo[:, :, t * P:(t + 1) * P], h2f[:, :, :], f(h2_hi[:, :, t * P:(t + 1) * P]),
                                ALU.subtract).then_inc(h2_lo_ready, 1)

            def up(n, j):
                dve.wait_ge(relu_ready, n + 1)
                r = relu_t[:, j % 2:j % 2 + 1, :]
                V.tensor_tensor(hid[:, ds(n, 1), :], r, r, ALU.mult).then_inc(hid_ready, 1)
                split_lo(U_UP + n + RING, j)

            def hidden_lo(n, j):
                dve.wait_ge(hd_hi_ready, n + 1)
                V.tensor_tensor(hd_lo[:, ds(j, 1), :], hid[:, ds(n, 1), :], f(hd_hi[:, ds(j, 1), :]),
                                ALU.subtract).then_inc(hd_lo_ready, 1)

            for n in range(2):
                up(n, n)
            with dve.Fori(0, FB // RING - 1) as q:
                for j in range(RING):
                    up(RING * q + j + 2, (j + 2) % RING)
            for j in range(RING):
                hidden_lo(j, j)
            for n in range(FB - 2, FB):
                up(n, n % RING)
            with dve.Fori(0, FB // RING - 1) as q:
                for j in range(RING):
                    hidden_lo(RING * q + j + RING, j)
                    split_lo(U_DOWN + RING * q + j + RING, j)
            for t in range(TB):
                for h in range(2):
                    cs = slice(h * HALF, (h + 1) * HALF)
                    dve.wait_ge(z_sq, 3 * t + h + 1)
                    wait(dve, z_out, 2 * t)
                    V.tensor_tensor(y2[:, cs], ps[:, 2 * t + h, :], modb[:, 3 * D + h * HALF:3 * D + (h + 1) * HALF],
                                    ALU.mult).then_inc(z_gained, 1)
                dve.wait_ge(z_sqrt, t + 1)
                V.reciprocal(stat[:, t:t + 1], stat[:, 12 + t:13 + t]).then_inc(z_rstd, 1)
                dve.wait_ge(z_rstd, t + 1)
                dve.wait_ge(z_gained, 2 * t + 2)
                for h in range(2):
                    cs = slice(h * HALF, (h + 1) * HALF)
                    V.scalar_tensor_tensor(xs[:, t, cs], y2[:, cs], stat[:, t:t + 1], xs[:, t, cs],
                                           ALU.mult, ALU.add).then_inc(z_out, 1)

        @block.tensor
        def _(pe):
            def column_unit(u, slot, r_hi, r_lo, bank):
                pe.wait_ge(w_lo_ready, split_count(u))
                for k in range(NB):
                    last = mm3(ps[:, bank, :], w_hi[:, slot, k * P:(k + 1) * P], w_lo[:, slot, k * P:(k + 1) * P],
                               r_hi[:, k, :], r_lo[:, k, :], k == 0, k == NB - 1)
                last.then_inc(unit_done, 1)

            pe.wait_ge(c_in, 16)
            pe.wait_ge(const_ready, 2)
            nc.tensor.transpose(ps[:, B_T0, 0:NB], crows[:, :], ident[0:NB, 0:NB]).then_inc(c_sum, 1)
            pe.wait_ge(vec_in, 16 * (len(vectors) + 2))
            nc.tensor.transpose(ps[:, B_T1, 0:NCOL], vrows[0:NCOL, :], ident[0:NCOL, 0:NCOL]).then_inc(cols_sum, 1)
            pe.wait_ge(cact, 1)
            for t in range(TB):
                pe.wait_ge(x_norm, t + 1)
                for k in range(NB):
                    if t == 0 and k == B_T1:
                        pe.wait_ge(cols_ready, 1)
                    last = nc.tensor.transpose(ps[:, k, t * P:(t + 1) * P], xs[:, t, k * P:(k + 1) * P], ident[:, :])
                    if t == TB - 1:
                        last.then_inc(x_tr, 1)

            def mod0_columns(j):
                pe.wait_ge(mod0_acc, NB * (j + 1))
                nc.tensor.matmul(ps[:, B_T1, 2 * j:2 * j + 1], mod0[:, 0, j * P:(j + 1) * P], ones[:, 0:1], start=True, stop=True)
                nc.tensor.matmul(ps[:, B_T1, 2 * j + 1:2 * j + 2], mod0[:, 1, j * P:(j + 1) * P], ones[:, 0:1],
                                 start=True, stop=True).then_inc(mod0_sum, 1)

            pe.wait_ge(xnt_ready, NB)
            pe.wait_ge(const_ready, 3)
            mod0_columns(0)
            for k in range(NB):
                if k + 1 < NB:
                    mod0_columns(k + 1)
                if k % 2 == 0:
                    pe.wait_ge(w0_lo_ready, k // 2 + 1)
                if k == 0:
                    pe.wait_ge(w_lo_ready, split_count(RING))
                pe.wait_ge(h_lo, k + 1)
                ks = slice(k * P, (k + 1) * P)
                for j in range(RING + 1):
                    bank, wh, wl = (j, w0_hi[:, j, ks], w0_lo[:, j, ks]) if j < RING else (B_T0, w_hi[:, 0, ks], w_lo[:, 0, ks])
                    last = mm3(ps[:, bank, :], wh, wl, ht_hi[:, k, :], ht_lo[:, k, :], k == 0, k == NB - 1)
                    if k == NB - 1:
                        last.then_inc(unit_done, 1)

            def gates(n):
                pe.wait_ge(xc_lo_ready, n + 1)
                pe.wait_ge(g_lo_ready, n + 1)
                wait(pe, r_ready, n)
                mm3(ps[:, B_R, :], g_hi[:, 0, :], g_lo[:, 0, :], xc_hi[:, :], xc_lo[:, :], True, True)
                wait(pe, i_ready, n)
                mm3(ps[:, B_I, :], g_hi[:, 1, :], g_lo[:, 1, :], xc_hi[:, :], xc_lo[:, :], True, True).then_inc(gates_done, 1)

            def mix(n, between):
                if not isinstance(n, int):
                    pe.wait_ge(xc_tap, n)
                    column_unit(4 * n, 0, ht_hi, ht_lo, 0)
                pe.wait_ge(c_copied, n)
                column_unit(4 * n + 1, 1, ht_hi, ht_lo, 1)
                between()
                pe.wait_ge(cv_ready, n)
                column_unit(4 * n + 2, 2, ht_hi, ht_lo, 2)
                pe.wait_ge(ya_f32, n)
                column_unit(4 * n + 3, 3, ht_hi, ht_lo, 3)
                gates(n)

            mix(1, lambda: gates(0))
            with pe.Fori(2, NB) as n:
                mix(n, lambda: None)

            def gate(n, bank_sems, before):
                u = U_GATE + 4 * n
                pe.wait_ge(bank_sems[0], n + before)
                column_unit(u, 0, ht_hi, ht_lo, 0)
                pe.wait_ge(bank_sems[1], n + before)
                column_unit(u + 1, 1, ht_hi, ht_lo, 1)
                pe.wait_ge(bank_sems[2], n + before)
                pe.wait_ge(ya_lo_ready, NB)
                column_unit(u + 2, 2, ya_hi, ya_lo, 2)
                pe.wait_ge(bank_sems[3], n + before)
                column_unit(u + 3, 3, ht_hi, ht_lo, 3)
                pe.wait_ge(mod_acc, 8 * (n + 1))
                wait(pe, mod_copied, n)
                nc.tensor.matmul(ps[:, B_T0, :], ones[:, :], modb[:, ds(n * HALF, HALF)], start=True, stop=True).then_inc(mod_sum, 1)

            gate(0, (xc_tap, c_copied, cv_ready, ya_f32), NB)
            with pe.Fori(1, NB) as n:
                gate(n, (gelu_ready, siga_ready, m_part, sigb_ready), 0)

            pe.wait_ge(yb_lo_ready, NB)
            for bank_sem in (gelu_ready, siga_ready, m_part, sigb_ready):
                pe.wait_ge(bank_sem, NB)
            for j in range(RING):
                column_unit(U_BOUT + j, j, yb_hi, yb_lo, j)
            with pe.Fori(1, NB // RING) as q:
                for j in range(RING):
                    pe.wait_ge(bout_scaled, RING * (q - 1) + j + 1)
                    column_unit(U_BOUT + RING * q + j, j, yb_hi, yb_lo, j)

            def transposes(t):
                pe.wait_ge(xn2_ready, t + 1)
                if t >= 2:
                    pe.wait_ge(h2_f32, NB * (t - 1))
                for k in range(NB):
                    last = nc.tensor.transpose(ps[:, B_R + k // 4 + 2 * (t % 2), (k % 4) * P:(k % 4 + 1) * P],
                                               xn2[:, k * P:(k + 1) * P], ident[:, :])
                last.then_inc(xn2_tr, 1)

            for t in range(TB):
                if t < 2:
                    pe.wait_ge(bout_scaled, NB - 2 + 2 * t)
                else:
                    pe.wait_ge(y_gained, 2 * (t - 1))
                for k in range(NB):
                    if t == 0:
                        pe.wait_ge(m_lo_ready, k + 1)
                        pe.wait_ge(w_lo_ready, split_count(U_WO + k))
                    wh, wl = (w_hi, w_lo) if k < RING else (wo2_hi, wo2_lo)
                    for h in range(2):
                        cs = slice(h * HALF, (h + 1) * HALF)
                        last = mm3(ps[:, 2 * (t % 2) + h, :], m_hi[:, k, t * P:(t + 1) * P], m_lo[:, k, t * P:(t + 1) * P],
                                   wh[:, k % RING, cs], wl[:, k % RING, cs], k == 0, k == NB - 1)
                    if t == TB - 1:
                        last.then_inc(unit_done, 1)
                if t < TB - 1:
                    last.then_inc(y_done, 1)
                if t >= 1:
                    transposes(t - 1)

            def up_first(tokens):
                for j in range(RING):
                    pe.wait_ge(w_lo_ready, split_count(U_UP + j))
                    if tokens.start == 0 and j == 2:
                        pe.wait_ge(y_gained, 2 * TB)
                    for k in range(NB):
                        last = mm3(ps[:, j, tokens], w_hi[:, j, k * P:(k + 1) * P], w_lo[:, j, k * P:(k + 1) * P],
                                   h2_hi[:, k, tokens], h2_lo[:, k, tokens], k == 0, k == NB - 1)
                    if tokens.start > 0:
                        last.then_inc(unit_done, 1)

            pe.wait_ge(h2_lo_ready, TB - 1)
            up_first(slice(0, (TB - 1) * P))
            transposes(TB - 1)

            def up_rest():
                pe.wait_ge(h2_lo_ready, TB)
                up_first(slice((TB - 1) * P, SEQ))

            up_rest()
            with pe.Fori(1, FB // RING) as q:
                for j in range(RING):
                    pe.wait_ge(relu_ready, RING * (q - 1) + j + 1)
                    column_unit(U_UP + RING * q + j, j, h2_hi, h2_lo, j)

            def down(slot, t, first, last, halves=range(2)):
                for h in halves:
                    cs = slice(h * HALF, (h + 1) * HALF)
                    mm = mm3(ps[:, 2 * t + h, :], hd_hi[:, slot, t * P:(t + 1) * P], hd_lo[:, slot, t * P:(t + 1) * P],
                             w_hi[:, slot, cs], w_lo[:, slot, cs], first, last)
                return mm

            def split_ready(n):
                pe.wait_ge(hd_lo_ready, n + 1)
                pe.wait_ge(w_lo_ready, split_count(U_DOWN + n))

            split_ready(0)
            for t in (2, 3, 0, 1):
                if t == 0:
                    pe.wait_ge(relu_ready, FB)
                mm = down(0, t, True, False)
            mm.then_inc(unit_done, 1)
            for n in range(1, RING):
                split_ready(n)
                for t in range(TB):
                    mm = down(n, t, False, False)
                mm.then_inc(unit_done, 1)
            with pe.Fori(1, FB // RING - 1) as q:
                for j in range(RING):
                    split_ready(RING * q + j)
                    for t in range(TB):
                        mm = down(j, t, False, False)
                    mm.then_inc(unit_done, 1)
            split_ready(FB - 1)
            for t in range(TB):
                for h in range(2):
                    for j in range(RING):
                        mm = down(j, t, False, j == RING - 1, (h,))
                    mm.then_inc(z_done, 1)


_INS = ['x', 'c', 'w_mod', 'b_mod', 'g_pre_mix', 'g_post_mix', 'w_in', 'conv_a_w', 'conv_a_b',
        'w_a_out', 'conv_b_w', 'conv_b_b', 'w_gate_r', 'b_gate_r', 'w_gate_i', 'b_gate_i',
        'lru_lambda', 'w_b_out', 'w_o', 'g_pre_mlp', 'g_post_mlp', 'w_mlp_up', 'w_mlp_down']
_OUTS = [((1, 512, 1024), 'float32')]


def kernel(**inputs):
    import numpy as _np
    import concourse.bacc as _bacc
    from concourse import mybir as _mybir
    from concourse.bass_utils import run_bass_kernel_spmd as _run

    nc = _bacc.Bacc("TRN2", target_bir_lowering=False, num_devices=1)
    arrays, args = {}, []
    for name in _INS:
        a = _np.ascontiguousarray(inputs[name])
        arrays[f"in_{name}_dram"] = a
        args.append(nc.dram_tensor(f"in_{name}_dram", a.shape, _mybir.dt.from_np(a.dtype), kind="ExternalInput").ap())
    for i, (shape, dtype) in enumerate(_OUTS):
        dt = _mybir.dt.from_np(_np.dtype(dtype))
        args.append(nc.dram_tensor(f"out_{i}_dram", shape, dt, kind="ExternalOutput").ap())
    hybrid_layer_kernel(nc, *args)
    r = _run(nc, [arrays], core_ids=[0])
    return r.results[0]["out_0_dram"]
```

```python
import concourse.bass as bass
from concourse import mybir
from contextlib import ExitStack


def hybrid_layer_kernel(nc, x, c, w_mod, b_mod, g_pre_mix, g_post_mix, w_in, conv_a_w, conv_a_b,
                        w_a_out, conv_b_w, conv_b_b, w_gate_r, b_gate_r, w_gate_i, b_gate_i,
                        lru_lambda, w_b_out, w_o, g_pre_mlp, g_post_mlp, w_mlp_up, w_mlp_down, out):
    f32 = mybir.dt.float32
    f32r = mybir.dt.float32r
    ALU = mybir.AluOpType
    ACT = mybir.ActivationFunctionType
    AX = mybir.AxisListType
    ds = bass.ds

    P = 128
    SEQ, D = x.shape[1], x.shape[2]
    NB = D // P
    TB = SEQ // P
    FB = w_mlp_up.shape[2] // P
    HALF = D // 2
    KA, KB = conv_a_w.shape[1], conv_b_w.shape[1]
    EPS = 1e-6
    LRU_C = 8.0
    RING = 4
    U_GATE, U_BOUT, U_WO, U_UP = 4 * NB, 8 * NB, 9 * NB, 10 * NB
    U_DOWN = U_UP + FB

    w_in_v = w_in[0].rearrange("(k p) n -> p k n", p=P)
    w_a_v = w_a_out[0].rearrange("(k p) n -> p k n", p=P)
    w_b_v = w_b_out[0].rearrange("(k p) n -> p k n", p=P)
    w_o_v = w_o[0].rearrange("(k p) n -> p k n", p=P)
    w_up_v = w_mlp_up[0].rearrange("(k p) n -> p k n", p=P)
    w_dn_v = w_mlp_down[0].rearrange("(k p) n -> p k n", p=P)
    w_mod_v = w_mod[0].rearrange("(k p) n -> p k n", p=P)
    x_v = x[0].rearrange("(t p) d -> p t d", p=P)
    out_v = out[0].rearrange("(t p) d -> p t d", p=P)
    COL_B, COL_C, COL_V, COL_XB, COL_G, COL_UA, COL_UB = [j * D for j in range(7)]

    ctx = ExitStack()
    with ctx:
        def sem(name):
            return ctx.enter_context(nc.semaphore(name))

        def sb(name, shape, dt=f32):
            return ctx.enter_context(nc.sbuf_tensor(name, shape, dt))

        ident = sb("ident", [P, P])
        ones = sb("ones", [P, P])
        cols = sb("cols", [P, P])
        s_mix = sb("s_mix", [P, NB])
        s_mlp = sb("s_mlp", [P, NB])
        mcol = sb("mcol", [P, 3 * NB])
        c_act = sb("c_act", [P, NB])
        k_neg = sb("k_neg", [P, NB])
        k_pos = sb("k_pos", [P, NB])
        sp = sb("sp", [P, 6, NB])
        stat = sb("stat", [P, 16])
        eps_t = sb("eps_t", [P, 1])
        ysum = sb("ysum", [P, 3 * TB])
        zsum = sb("zsum", [P, 3 * TB])

        KIB = 1024
        ROW = SEQ * 4
        base = (nc.sbuf_base + 31) // 32 * 32
        room = nc.sbuf_usable_end - base - 512
        arena_bytes = 204 * KIB
        assert arena_bytes <= room, (arena_bytes, room)
        arena = ctx.enter_context(nc.sbuf_tensor("arena", [P, arena_bytes // 4], f32))
        O_XS, O_HT, O_YA, O_YB, O_RING, O_RAW, O_HM, O_MB, O_MR, O_GS = [
            base + KIB * k for k in (0, 16, 48, 80, 112, 144, 160, 176, 192, 200)]

        def at(name, shape, off, dt=f32):
            return nc.alloc_sbuf_tensor_at(name, shape, dt, offset=off)

        xs = at("xs", [P, TB, D], O_XS)
        sig_b = at("sig_b", [P, NB, SEQ], O_XS)
        ht_hi = at("ht_hi", [P, NB, SEQ], O_HT, f32r)
        ht_lo = at("ht_lo", [P, NB, SEQ], O_HT + 16 * KIB, f32r)
        wo2_hi = at("wo2_hi", [P, RING, D], O_HT, f32r)
        wo2_lo = at("wo2_lo", [P, RING, D], O_HT + 16 * KIB, f32r)
        ya_hi = at("ya_hi", [P, NB, SEQ], O_YA, f32r)
        ya_lo = at("ya_lo", [P, NB, SEQ], O_YA + 16 * KIB, f32r)
        m_hi = at("m_hi", [P, NB, SEQ], O_YA, f32r)
        m_lo = at("m_lo", [P, NB, SEQ], O_YA + 16 * KIB, f32r)
        hid = at("hid", [P, FB, SEQ], O_HT)
        yb_hi = at("yb_hi", [P, NB, SEQ], O_YB, f32r)
        yb_lo = at("yb_lo", [P, NB, SEQ], O_YB + 16 * KIB, f32r)
        h2_hi = at("h2_hi", [P, NB, SEQ], O_YB, f32r)
        h2_lo = at("h2_lo", [P, NB, SEQ], O_YB + 16 * KIB, f32r)
        w_hi = at("w_hi", [P, RING, D], O_RING, f32r)
        w_lo = at("w_lo", [P, RING, D], O_RING + 16 * KIB, f32r)
        raw = at("raw", [P, RING, D], O_RAW)
        xnt = at("xnt", [P, NB, SEQ], O_HM)
        hm = at("hm", [P, NB, SEQ], O_HM)
        modb = at("modb", [P, 4 * D], O_MB)
        modb_lo = at("modb_lo", [P, 4 * D], O_MB, f32r)
        modb_hi = at("modb_hi", [P, HALF], O_XS + (NB - 1) * ROW, f32r)
        modb_hi_last = at("modb_hi_last", [P, HALF], O_HT, f32r)
        modraw = at("modraw", [P, 2, 2, HALF], O_MR)
        g_bc = at("g_bc", [P, 2, D], O_MR)
        gel = at("gel", [P, SEQ], O_GS)
        sig_a = at("sig_a", [P, SEQ], O_GS + ROW)
        picked = at("picked", [P, HALF // P, P], O_GS)[:, :, :]
        M0_BUFS = 3
        mod0_raw = at("mod0_raw", [P, M0_BUFS, NB // 2, 2, 2 * P], O_YB)
        mod0 = at("mod0", [P, 2, D], O_YB + 24 * KIB)
        vrows = at("vrows", [P, P], O_MB)
        crows = at("crows", [NB, P], O_MB + KIB)
        raw0 = at("raw0", [P, RING, D], O_YA)
        w0_hi = at("w0_hi", [P, RING, D], O_XS, f32r)
        w0_lo = at("w0_lo", [P, RING, D], O_MB, f32r)
        xc, xc_hi, xc_lo, c_sb, ca, r_t, i_t, t_t, a_t, q_t = [
            at(nm, [P, SEQ], O_YB + ROW * k, f32r if nm in ("xc_hi", "xc_lo") else f32)
            for k, nm in enumerate("xc xc_hi xc_lo c_sb ca r_t i_t t_t a_t q_t".split())]
        g_hi = at("g_hi", [P, 2, P], O_YB + 20 * KIB, f32r)
        g_lo = at("g_lo", [P, 2, P], O_YB + 21 * KIB, f32r)
        graw = at("graw", [P, 2, P], O_YB + 22 * KIB)
        xbp = at("xbp", [P, KB - 1 + SEQ], O_YB + 25 * KIB)
        cvp = at("cvp", [P, KA - 1 + SEQ], O_YB + 28 * KIB)
        y1 = at("y1", [P, D], O_HM)
        xn2 = at("xn2", [P, D], O_HM + 4 * KIB)
        h2f = at("h2f", [P, NB, P], O_HM + 8 * KIB)
        junk = at("junk", [P, D], O_HM + 12 * KIB)
        junk0 = at("junk0", [P, D], O_GS)
        relu_t = at("relu_t", [P, 2, SEQ], O_GS)
        hd_hi = at("hd_hi", [P, RING, SEQ], O_HM, f32r)
        hd_lo = at("hd_lo", [P, RING, SEQ], O_HM + 8 * KIB, f32r)
        y2 = at("y2", [P, D], O_MR)
        junk2 = at("junk2", [P, D], O_GS)

        ps = ctx.enter_context(nc.psum_tensor("ps", [P, 8, HALF], f32))
        B_R, B_I, B_T0, B_T1 = 4, 5, 6, 7

        C_GX, C_GM, C_AW, C_AB, C_BW = 0, NB, 2 * NB, (2 + KA) * NB, (3 + KA) * NB
        C_BB = C_BW + KB * NB
        C_BR, C_BI, C_LAM = C_BB + NB, C_BB + 2 * NB, C_BB + 3 * NB
        C_BS, C_BC = C_LAM + NB, C_LAM + 2 * NB
        NCOL = C_BC + NB
        vectors = [(C_GX, g_pre_mix[0]), (C_GM, g_pre_mlp[0]), (C_AB, conv_a_b[0]),
                   (C_BB, conv_b_b[0]), (C_BR, b_gate_r[0]), (C_BI, b_gate_i[0]), (C_LAM, lru_lambda[0]),
                   (C_BS, b_mod[0, 0:D]), (C_BC, b_mod[0, D:2 * D])]
        vectors = [(off, vec.rearrange("(b p) -> b p", p=P)) for off, vec in vectors]
        vectors += [(C_AW, conv_a_w[0].rearrange("k (b p) -> (k b) p", p=P)),
                    (C_BW, conv_b_w[0].rearrange("k (b p) -> (k b) p", p=P))]

        c_in = sem("c_in")
        vec_in = sem("vec_in")
        vec_pool_in = sem("vec_pool_in")
        xr_in0 = sem("xr_in0")
        xr_in1 = sem("xr_in1")
        xr_in2 = sem("xr_in2")
        xr_in3 = sem("xr_in3")
        mod0_in0 = sem("mod0_in0")
        mod0_in1 = sem("mod0_in1")
        mod0_in2 = sem("mod0_in2")
        raw0a_in = sem("raw0a_in")
        raw0b_in = sem("raw0b_in")
        raw0c_in = sem("raw0c_in")
        raw_in0 = sem("raw_in0")
        raw_in1 = sem("raw_in1")
        raw_in2 = sem("raw_in2")
        raw_in3 = sem("raw_in3")
        graw_in = sem("graw_in")
        modraw_in0 = sem("modraw_in0")
        modraw_in1 = sem("modraw_in1")
        bmod_in = sem("bmod_in")
        gbc_in = sem("gbc_in")
        out_done = sem("out_done")
        loads_begun = sem("loads_begun")
        const_ready = sem("const_ready")
        zeromb_ready = sem("zeromb_ready")
        c_sum = sem("c_sum")
        sig_c = sem("sig_c")
        cact = sem("cact")
        cols_sum = sem("cols_sum")
        cols_ready = sem("cols_ready")
        sp_act = sem("sp_act")
        sp_step = sem("sp_step")
        x_sq = sem("x_sq")
        x_sqrt = sem("x_sqrt")
        x_rstd = sem("x_rstd")
        x_norm = sem("x_norm")
        x_tr = sem("x_tr")
        xnt_ready = sem("xnt_ready")
        xnt_ready_dve = sem("xnt_ready_dve")
        mod0_acc = sem("mod0_acc")
        mod0_sum = sem("mod0_sum")
        col0_ready = sem("col0_ready")
        h_f32 = sem("h_f32")
        h_hi = sem("h_hi")
        h_lo = sem("h_lo")
        w0_hi_ready = sem("w0_hi_ready")
        w0_lo_ready = sem("w0_lo_ready")
        w_hi_ready = sem("w_hi_ready")
        w_lo_ready = sem("w_lo_ready")
        unit_done = sem("unit_done")
        xb_copied = sem("xb_copied")
        xc_tap = sem("xc_tap")
        xc_conv = sem("xc_conv")
        xc_hi_ready = sem("xc_hi_ready")
        xc_lo_ready = sem("xc_lo_ready")
        g_hi_ready = sem("g_hi_ready")
        g_lo_ready = sem("g_lo_ready")
        gates_done = sem("gates_done")
        r_ready = sem("r_ready")
        i_ready = sem("i_ready")
        t_ready = sem("t_ready")
        a_ready = sem("a_ready")
        q_ready = sem("q_ready")
        q2_ready = sem("q2_ready")
        mult_ready = sem("mult_ready")
        ix_ready = sem("ix_ready")
        bx_ready = sem("bx_ready")
        scan_ready = sem("scan_ready")
        c_copied = sem("c_copied")
        cv_ready = sem("cv_ready")
        ca_tap = sem("ca_tap")
        ca_conv = sem("ca_conv")
        ya_f32 = sem("ya_f32")
        ya_hi_ready = sem("ya_hi_ready")
        ya_lo_ready = sem("ya_lo_ready")
        gelu_ready = sem("gelu_ready")
        yb_f32 = sem("yb_f32")
        yb_hi_ready = sem("yb_hi_ready")
        yb_lo_ready = sem("yb_lo_ready")
        siga_ready = sem("siga_ready")
        m_part = sem("m_part")
        sigb_ready = sem("sigb_ready")
        mod_acc = sem("mod_acc")
        mod_hi_ready = sem("mod_hi_ready")
        mod_lo_ready = sem("mod_lo_ready")
        mod_sum = sem("mod_sum")
        mod_copied = sem("mod_copied")
        diag_step = sem("diag_step")
        colf_ready = sem("colf_ready")
        gm_ready = sem("gm_ready")
        bout_scaled = sem("bout_scaled")
        m_f32 = sem("m_f32")
        m_hi_ready = sem("m_hi_ready")
        m_lo_ready = sem("m_lo_ready")
        y_done = sem("y_done")
        y_sq = sem("y_sq")
        y_sqrt = sem("y_sqrt")
        y_gained = sem("y_gained")
        y_rstd = sem("y_rstd")
        x1_ready = sem("x1_ready")
        x1_sq = sem("x1_sq")
        x1_sqrt = sem("x1_sqrt")
        x1_rstd = sem("x1_rstd")
        xn2_ready = sem("xn2_ready")
        xn2_tr = sem("xn2_tr")
        h2_f32 = sem("h2_f32")
        h2_f32_dve = sem("h2_f32_dve")
        h2_hi_ready = sem("h2_hi_ready")
        h2_lo_ready = sem("h2_lo_ready")
        relu_ready = sem("relu_ready")
        hid_ready = sem("hid_ready")
        hd_hi_ready = sem("hd_hi_ready")
        hd_lo_ready = sem("hd_lo_ready")
        z_done = sem("z_done")
        z_sq = sem("z_sq")
        z_sqrt = sem("z_sqrt")
        z_gained = sem("z_gained")
        z_rstd = sem("z_rstd")
        z_out = sem("z_out")
        raw_in = [raw_in0, raw_in1, raw_in2, raw_in3]
        xr_in = [xr_in0, xr_in1, xr_in2, xr_in3]
        mod0_in = [mod0_in0, mod0_in1, mod0_in2]
        modraw_in = [modraw_in0, modraw_in1]

        SP_STEPS = 16
        WO_ORDER = [0, 1, RING, 2, RING + 1, 3, RING + 2, RING + 3]

        def wo_count(k):
            return split_count(U_WO) + WO_ORDER.index(k)

        def split_count(u):
            return u - RING + 1

        def wait(eng, semaphore, count):
            if not isinstance(count, int) or count > 0:
                eng.wait_ge(semaphore, count)

        def mm3(dst, l_hi, l_lo, r_hi, r_lo, first, last):
            nc.tensor.matmul(dst, l_hi, r_hi, start=first, stop=False)
            nc.tensor.matmul(dst, l_hi, r_lo, start=False, stop=False)
            return nc.tensor.matmul(dst, l_lo, r_hi, start=False, stop=last)

        def load_vectors(eng, some, semaphore):
            for off, rows in some:
                eng.dma_start(vrows[off:off + rows.shape[0], :], rows).then_inc(semaphore, 16)

        block = ctx.enter_context(nc.Block())

        @block.sync
        def _(sp_eng):
            def load_unit(u, slot, src):
                wait(sp_eng, w_lo_ready, split_count(u - RING))
                sp_eng.sem_inc(loads_begun, 1)
                dst = raw[:, slot, :]
                if len(src.shape) == 3:
                    dst = dst.rearrange("p (k n) -> p k n", k=NB)
                sp_eng.dma_start(dst, src).then_inc(raw_in[slot], 16)

            def load_gates(n):
                wait(sp_eng, g_lo_ready, n)
                sp_eng.dma_start(graw[:, 0, :], w_gate_r[0, ds(n, 1)].rearrange("a p j -> p (a j)")).then_inc(graw_in, 16)
                sp_eng.dma_start(graw[:, 1, :], w_gate_i[0, ds(n, 1)].rearrange("a p j -> p (a j)")).then_inc(graw_in, 16)

            def load_mod0(i):
                wait(sp_eng, mod0_acc, NB // 2 * (i - M0_BUFS + 1))
                ks = slice(i % 2 * NB // 2, (i % 2 + 1) * NB // 2)
                for a in range(2):
                    col = a * D + i // 2 * 2 * P
                    sp_eng.dma_start(mod0_raw[:, i % M0_BUFS, :, a, :],
                                     w_mod_v[:, ks, col:col + 2 * P]).then_inc(mod0_in[i % M0_BUFS], 16)

            def load_first_units(ks, semaphore):
                for j, col in enumerate((COL_XB, COL_C, COL_V, COL_B)):
                    sp_eng.dma_start(raw0[:, j, :].rearrange("p (k n) -> p k n", k=NB)[:, ks, :],
                                     w_in_v[:, ks, col:col + P]).then_inc(semaphore, 16)

            load_mod0(0)
            for t in range(TB):
                sp_eng.dma_start(xs[:, t, :], x_v[:, t, :]).then_inc(xr_in[t], 16)
                if t == 0:
                    load_vectors(sp_eng, vectors[1::3], vec_in)
            load_mod0(1)
            load_first_units(slice(0, 2), raw0a_in)
            load_unit(RING, 0, w_in_v[:, :, COL_XB + P:COL_XB + 2 * P])
            load_mod0(2)
            load_mod0(3)
            load_first_units(slice(2, 4), raw0b_in)
            load_mod0(4)
            load_mod0(5)
            load_first_units(slice(4, NB), raw0c_in)
            load_mod0(6)
            load_mod0(7)
            load_unit(RING + 1, 1, w_in_v[:, :, COL_C + P:COL_C + 2 * P])
            load_unit(RING + 2, 2, w_in_v[:, :, COL_V + P:COL_V + 2 * P])
            load_unit(RING + 3, 3, w_in_v[:, :, COL_B + P:COL_B + 2 * P])
            sp_eng.wait_ge(mod0_acc, NB // 2 * NB)
            load_gates(0)

            with sp_eng.Fori(2, NB) as n:
                for j, col in enumerate((COL_XB, COL_C, COL_V, COL_B)):
                    load_unit(4 * n + j, j, w_in_v[:, :, ds(col + n * P, P)])
                    if j == 0:
                        load_gates(n - 1)
            load_gates(NB - 1)

            gate_cols = ((w_in_v, COL_G), (w_in_v, COL_UA), (w_a_v, 0), (w_in_v, COL_UB))
            b_cols = tuple((w_b_v, j * P) for j in range(RING))
            for j, (view, col) in enumerate(gate_cols):
                load_unit(U_GATE + j, j, view[:, :, ds(col, P)])

            def mod_and_next(n, nxt, nxt_cols):
                for j, (view, col) in enumerate(nxt_cols):
                    wait(sp_eng, mod_acc, 8 * n + 2 * j - 2)
                    sp_eng.sem_inc(loads_begun, 1)
                    sp_eng.dma_start(modraw[:, j % 2, :, :],
                                     w_mod_v[:, 2 * j:2 * j + 2, ds(2 * D + n * HALF, HALF)]).then_inc(modraw_in[j % 2], 16)
                    load_unit(U_GATE + 4 * n + 4 + j, j, view[:, :, ds(col + nxt * P, P)])

            mod_and_next(0, 1, gate_cols)
            with sp_eng.Fori(1, NB - 1) as n:
                mod_and_next(n, n + 1, gate_cols)
            mod_and_next(NB - 1, 0, b_cols)
            for j in range(RING):
                load_unit(U_BOUT + RING + j, j, w_b_v[:, :, (RING + j) * P:(RING + j + 1) * P])
            sp_eng.wait_ge(mod_acc, 8 * NB)
            sp_eng.dma_start(g_bc[:, 0, :], g_post_mix[0:1, :].to_broadcast([P, D])).then_inc(gbc_in, 16)
            sp_eng.dma_start(g_bc[:, 1, :], g_post_mlp[0:1, :].to_broadcast([P, D])).then_inc(gbc_in, 16)
            for k in range(NB):
                if k >= RING:
                    sp_eng.wait_ge(w_lo_ready, wo_count(k - RING))
                load_unit(U_WO + k, k % RING, w_o_v[:, k, :])
            sp_eng.wait_ge(m_f32, NB)
            for t in range(TB):
                sp_eng.dma_start(xs[:, t, :], x_v[:, t, :]).then_inc(xr_in[t], 16)

            with sp_eng.Fori(0, FB // RING) as q:
                for j in range(RING):
                    load_unit(U_UP + RING * q + j, j, w_up_v[:, :, ds((RING * q + j) * P, P)])
            with sp_eng.Fori(0, FB // RING) as q:
                for j in range(RING):
                    load_unit(U_DOWN + RING * q + j, j, w_dn_v[:, ds(RING * q + j, 1), :].rearrange("p a n -> p (a n)"))
            for t in range(TB):
                for h in range(2):
                    sp_eng.wait_ge(z_out, 2 * t + h + 1)
                    sp_eng.dma_start(out_v[:, t, h * HALF:(h + 1) * HALF],
                                     xs[:, t, h * HALF:(h + 1) * HALF]).then_inc(out_done, 16)
            sp_eng.wait_ge(out_done, 16 * 2 * TB)

        @block.gpsimd
        def _(pool):
            nc.gpsimd.memset(ident[:, :], 0.0).then_inc(const_ready, 1)
            pool.wait_ge(const_ready, 1)
            nc.gpsimd.affine_select(out=ident[:, :], in_=ident[:, :], compare_op=ALU.not_equal, fill=1.0,
                                    base=0, pattern=[[-1, P]], channel_multiplier=1).then_inc(const_ready, 1)
            nc.gpsimd.memset(ones[:, :], 1.0).then_inc(const_ready, 1)
            nc.gpsimd.memset(eps_t[:, :], EPS).then_inc(const_ready, 1)
            load_vectors(pool, vectors[0::3], vec_pool_in)
            pool.wait_ge(cols_sum, 1)
            for q in range(NB // 2):
                pool.wait_ge(w0_hi_ready, q + 1)
                cs = slice(2 * q * P, 2 * (q + 1) * P)
                nc.gpsimd.tensor_tensor(w0_lo[:, :, cs], raw0[:, :, cs], w0_hi[:, :, cs].bitcast(f32),
                                        ALU.subtract).then_inc(w0_lo_ready, 1)
                if q == 0:
                    pool.wait_ge(w_hi_ready, split_count(RING))
                    nc.gpsimd.tensor_tensor(w_lo[:, 0, :], raw[:, 0, :], w_hi[:, 0, :].bitcast(f32),
                                            ALU.subtract).then_inc(w_lo_ready, 1)
            pool.wait_ge(mod0_sum, NB // 2)
            nc.gpsimd.memset(xbp[:, 0:KB - 1], 0.0).then_inc(const_ready, 1)
            nc.gpsimd.memset(cvp[:, 0:KA - 1], 0.0).then_inc(const_ready, 1)
            pool.wait_ge(unit_done, RING)
            nc.gpsimd.memset(modb[:, :], 0.0).then_inc(zeromb_ready, 1)
            pool.wait_ge(zeromb_ready, 1)
            pool.dma_start(modb[0:1, :], b_mod[0:1, 2 * D:6 * D]).then_inc(bmod_in, 16)

        @block.scalar
        def _(act):
            A = nc.scalar.activation

            def split_hi(u, slot, u_free=None):
                if u_free is None:
                    u_free = 0 if isinstance(u, int) and u < 2 * RING else u - RING + 1
                wait(act, unit_done, u_free)
                act.wait_ge(raw_in[slot], 16 * (u // RING))
                A(w_hi[:, slot, :], raw[:, slot, :], ACT.Copy).then_inc(w_hi_ready, 1)

            act.dma_start(crows[:, :], c[0].rearrange("(b p) -> b p", p=P)).then_inc(c_in, 16)
            load_vectors(act, vectors[2::3], vec_in)

            act.wait_ge(c_sum, 1)
            A(c_act[:, :], ps[:, B_T0, 0:NB], ACT.Sigmoid).then_inc(sig_c, 1)
            act.wait_ge(const_ready, 4)
            for t in range(TB):
                act.wait_ge(xr_in[t], 16)
                wait(act, x_sq, t)
                A(junk0[:, :], xs[:, t, :], ACT.Square, accum_out=stat[:, t:t + 1]).then_inc(x_sq, 1)
                act.wait_ge(x_sq, t + 1)
                A(stat[:, 4 + t:5 + t], stat[:, t:t + 1], ACT.Sqrt, scale=1.0 / D, bias=eps_t[:, 0:1]).then_inc(x_sqrt, 1)
            act.wait_ge(sp_step, 1)
            A(sp[:, 1, :], sp[:, 0, :], ACT.Exp).then_inc(sp_act, 1)

            def first_units_hi(q):
                cs = slice(2 * q * P, 2 * (q + 1) * P)
                A(w0_hi[:, :, cs], raw0[:, :, cs], ACT.Copy).then_inc(w0_hi_ready, 1)

            act.wait_ge(x_tr, NB)
            for k in (NB - 1, 0, 1, 2):
                A(xnt[:, k, :], ps[:, k, :], ACT.Copy).then_inc(xnt_ready, 1)
                if k == NB - 1:
                    act.wait_ge(raw0a_in, 16 * RING)
                    first_units_hi(0)
            act.wait_ge(xnt_ready, 4)
            for k in range(NB):
                act.wait_ge(col0_ready, 3 * (k // 2 + 1))
                if k == 3:
                    act.wait_ge(xnt_ready_dve, 4)
                A(xnt[:, k, :], xnt[:, k, :], ACT.Identity, scale=s_mix[:, k:k + 1], bias=mcol[:, k:k + 1]).then_inc(h_f32, 1)
                act.wait_ge(h_f32, k + 1)
                A(ht_hi[:, k, :], xnt[:, k, :], ACT.Copy).then_inc(h_hi, 1)
                if k == 0:
                    split_hi(RING, 0)
                if k == 1:
                    act.wait_ge(raw0b_in, 16 * RING)
                    first_units_hi(1)
                if k == 3 or k == 4:
                    act.wait_ge(raw0c_in, 16 * RING)
                    first_units_hi(k - 1)
            split_hi(RING + 1, 1)

            def split_gates(n):
                wait(act, gates_done, n)
                act.wait_ge(graw_in, 32 * (n + 1))
                A(g_hi[:, :, :], graw[:, :, :], ACT.Copy).then_inc(g_hi_ready, 1)

            def recurrence(n):
                act.wait_ge(gates_done, n + 1)
                A(r_t[:, :], ps[:, B_R, :], ACT.Sigmoid, bias=cols[:, ds(C_BR + n, 1)]).then_inc(r_ready, 1)
                A(i_t[:, :], ps[:, B_I, :], ACT.Sigmoid, bias=cols[:, ds(C_BI + n, 1)]).then_inc(i_ready, 1)
                act.wait_ge(r_ready, n + 1)
                A(t_t[:, :], r_t[:, :], ACT.Tanh, scale=k_pos[:, ds(n, 1)]).then_inc(t_ready, 1)
                A(a_t[:, :], r_t[:, :], ACT.Exp, scale=k_neg[:, ds(n, 1)]).then_inc(a_ready, 1)
                act.wait_ge(a_ready, n + 1)
                A(q_t[:, :], a_t[:, :], ACT.Square).then_inc(q_ready, 1)

            def recurrence_root(n):
                act.wait_ge(q2_ready, n + 1)
                A(q_t[:, :], q_t[:, :], ACT.Sqrt).then_inc(mult_ready, 1)

            def mix(n, after_xb, splits, xb_bank=0):
                act.wait_ge(unit_done, 4 * n + 1)
                wait(act, xc_conv, 3 * n)
                A(xbp[:, KB - 1:], ps[:, xb_bank, :], ACT.Copy).then_inc(xb_copied, 1)
                wait(act, ix_ready, n)
                A(xc[:, :], ps[:, xb_bank, :], ACT.Identity, scale=cols[:, ds(C_BW + (KB - 1) * NB + n, 1)],
                  bias=cols[:, ds(C_BB + n, 1)]).then_inc(xc_tap, 1)
                first = isinstance(n, int) and n == 0
                if first:
                    act.wait_ge(unit_done, 2)
                    A(c_sb[:, :], ps[:, 1, :], ACT.Copy).then_inc(c_copied, 1)
                if splits[0] is not None:
                    split_hi(splits[0], splits[0] % RING if isinstance(n, int) else 0)
                after_xb()
                wait(act, gates_done, n)
                act.wait_ge(xc_conv, 3 * (n + 1))
                A(xc_hi[:, :], xc[:, :], ACT.Copy).then_inc(xc_hi_ready, 1)
                split_gates(n)
                if not first:
                    act.wait_ge(unit_done, 4 * n + 2)
                    wait(act, cv_ready, n)
                    A(c_sb[:, :], ps[:, 1, :], ACT.Copy).then_inc(c_copied, 1)
                if splits[1] is not None:
                    split_hi(splits[1], splits[1] % RING if isinstance(n, int) else 1)
                act.wait_ge(cv_ready, n + 1)
                wait(act, ya_lo_ready, n)
                A(ca[:, :], cvp[:, KA - 1:], ACT.Identity, scale=cols[:, ds(C_AW + (KA - 1) * NB + n, 1)],
                  bias=cols[:, ds(C_AB + n, 1)]).then_inc(ca_tap, 1)
                if splits[2] is not None:
                    split_hi(splits[2], splits[2] % RING if isinstance(n, int) else 2)
                act.wait_ge(ya_f32, n + 1)
                A(ya_hi[:, ds(n, 1), :], ca[:, None, :], ACT.Copy).then_inc(ya_hi_ready, 1)
                if splits[3] is not None:
                    split_hi(splits[3], splits[3] % RING if isinstance(n, int) else 3)

            act.wait_ge(const_ready, 6)
            act.wait_ge(sp_step, SP_STEPS + 1)
            mix(0, lambda: None, (RING + 2, RING + 3, RING + 4, None))
            recurrence(0)
            mix(1, lambda: recurrence_root(0), (None,) + tuple(2 * RING + j for j in range(1, RING)), B_T0)
            with act.Fori(2, NB) as n:
                split_hi(4 * n + RING, 0)
                recurrence(n - 1)
                mix(n, lambda: recurrence_root(n - 1), (None,) + tuple(4 * n + RING + j for j in range(1, RING)))
            recurrence(NB - 1)

            def mod_hi(n, hi):
                A(hi[:, :], modb[:, ds(n * HALF, HALF)], ACT.Copy).then_inc(mod_hi_ready, 1)

            def mod_columns(n):
                A(modb[:, ds(n * HALF, HALF)], ps[:, B_T0, :], ACT.Copy).then_inc(mod_copied, 1)

            def gate(n):
                later = not isinstance(n, int)
                act.wait_ge(unit_done, U_GATE + 4 * n + 1)
                wait(act, yb_lo_ready, n)
                A(gel[:, :], ps[:, 0, :], ACT.Gelu_apprx_tanh).then_inc(gelu_ready, 1)
                if later:
                    act.wait_ge(mod_acc, 8 * n)
                split_hi(U_GATE + 4 * n + 4, 0)
                if later:
                    mod_hi(n - 1, modb_hi)
                act.wait_ge(unit_done, U_GATE + 4 * n + 2)
                wait(act, m_part, n)
                A(sig_a[:, :], ps[:, 1, :], ACT.Sigmoid).then_inc(siga_ready, 1)
                split_hi(U_GATE + 4 * n + 5, 1)
                act.wait_ge(yb_f32, n + 1)
                A(yb_hi[:, ds(n, 1), :], gel[:, None, :], ACT.Copy).then_inc(yb_hi_ready, 1)
                split_hi(U_GATE + 4 * n + 6, 2)
                act.wait_ge(unit_done, U_GATE + 4 * n + 4)
                A(sig_b[:, ds(n, 1), :], ps[:, 3:4, :], ACT.Sigmoid).then_inc(sigb_ready, 1)
                if later:
                    act.wait_ge(mod_sum, n)
                split_hi(U_GATE + 4 * n + 7, 3)
                if later:
                    mod_columns(n - 1)

            recurrence_root(NB - 1)
            act.wait_ge(scan_ready, NB)
            gate(0)
            with act.Fori(1, NB) as n:
                gate(n)

            act.wait_ge(mod_acc, 8 * NB)
            mod_hi(NB - 1, modb_hi_last)
            act.wait_ge(mod_sum, NB)
            mod_columns(NB - 1)

            def w_o_hi(k):
                j = k % RING
                if k >= RING:
                    act.wait_ge(unit_done, U_BOUT + k + 1)
                act.wait_ge(raw_in[j], 16 * ((U_WO + k) // RING))
                A((wo2_hi if k < RING else w_hi)[:, j, :], raw[:, j, :], ACT.Copy).then_inc(w_hi_ready, 1)

            for n in range(NB):
                if n >= RING:
                    w_o_hi(n - RING)
                if n > RING:
                    w_o_hi(n - 1)
                act.wait_ge(m_f32, n + 1)
                A(m_hi[:, n, :], hm[:, n, :], ACT.Copy).then_inc(m_hi_ready, 1)
                if n < RING:
                    split_hi(U_BOUT + n + RING, n)
            w_o_hi(NB - 1)

            def y_squares(t):
                if t < TB - 1:
                    act.wait_ge(y_done, t + 1)
                else:
                    act.wait_ge(unit_done, U_UP)
                for h in range(2):
                    A(junk[:, h * HALF:(h + 1) * HALF], ps[:, 2 * (t % 2) + h, :], ACT.Square,
                      accum_out=ysum[:, 2 * t + h:2 * t + h + 1]).then_inc(y_sq, 1)
                    if h == 0:
                        act.wait_ge(y_sq, 3 * t + 1)
                        A(ysum[:, 2 * TB + t:2 * TB + t + 1], ysum[:, 2 * t:2 * t + 1], ACT.Identity, scale=1.0 / D,
                          bias=eps_t[:, 0:1]).then_inc(y_sq, 1)
                act.wait_ge(y_sq, 3 * t + 3)
                A(stat[:, 12:13], ysum[:, 2 * t + 1:2 * t + 2], ACT.Sqrt, scale=1.0 / D,
                  bias=ysum[:, 2 * TB + t:2 * TB + t + 1]).then_inc(y_sqrt, 1)

            def up_split_hi(j):
                split_hi(U_UP + j, j, U_WO + j + 1)

            for t in range(TB):
                y_squares(t)
                if t == TB - 2:
                    up_split_hi(0)
                if t == TB - 1:
                    up_split_hi(3)
                act.wait_ge(x1_ready, t + 1)
                A(junk[:, :], xs[:, t, :], ACT.Square, accum_out=stat[:, t:t + 1]).then_inc(x1_sq, 1)
                act.wait_ge(x1_sq, t + 1)
                A(stat[:, 13:14], stat[:, t:t + 1], ACT.Sqrt, scale=1.0 / D, bias=eps_t[:, 0:1]).then_inc(x1_sqrt, 1)
                if t == TB - 2:
                    up_split_hi(1)
                    up_split_hi(2)
                if t == 0:
                    act.wait_ge(colf_ready, 1)
                act.wait_ge(xn2_tr, t + 1)
                wait(act, h2_lo_ready, 2 * t)
                for k in range(NB // 2):
                    A(h2f[:, k, :], ps[:, B_R + 2 * (t % 2), k * P:(k + 1) * P], ACT.Identity,
                      scale=s_mlp[:, k:k + 1], bias=mcol[:, NB + k:NB + k + 1]).then_inc(h2_f32, 1)
                for part, semaphore in enumerate((h2_f32, h2_f32_dve)):
                    act.wait_ge(semaphore, NB // 2 * (t + 1))
                    ks = slice(part * NB // 2, (part + 1) * NB // 2)
                    A(h2_hi[:, ks, t * P:(t + 1) * P], h2f[:, ks, :], ACT.Copy).then_inc(h2_hi_ready, 1)

            def up(n, j):
                act.wait_ge(unit_done, U_UP + n + 1)
                wait(act, hid_ready, n - 1)
                A(relu_t[:, j % 2, :], ps[:, j, :], ACT.Relu).then_inc(relu_ready, 1)
                split_hi(U_UP + n + RING, j)

            def hidden_hi(n, j):
                if not isinstance(n, int):
                    act.wait_ge(unit_done, U_DOWN + n - RING + 1)
                act.wait_ge(hid_ready, n + 1)
                A(hd_hi[:, ds(j, 1), :], hid[:, ds(n, 1), :], ACT.Copy).then_inc(hd_hi_ready, 1)

            for n in range(2):
                up(n, n)
            with act.Fori(0, FB // RING - 1) as q:
                for j in range(RING):
                    up(RING * q + j + 2, (j + 2) % RING)
            for j in range(RING):
                hidden_hi(j, j)
            for n in range(FB - 2, FB):
                up(n, n % RING)

            with act.Fori(0, FB // RING - 1) as q:
                for j in range(RING):
                    hidden_hi(RING * q + j + RING, j)
                    split_hi(U_DOWN + RING * q + j + RING, j)

            for t in range(TB):
                for h in range(2):
                    act.wait_ge(z_done, 2 * t + h + 1)
                    A(junk2[:, h * HALF:(h + 1) * HALF], ps[:, 2 * t + h, :], ACT.Square,
                      accum_out=zsum[:, 2 * t + h:2 * t + h + 1]).then_inc(z_sq, 1)
                    if h == 0:
                        act.wait_ge(z_sq, 3 * t + 1)
                        A(zsum[:, 2 * TB + t:2 * TB + t + 1], zsum[:, 2 * t:2 * t + 1], ACT.Identity, scale=1.0 / D,
                          bias=eps_t[:, 0:1]).then_inc(z_sq, 1)
                act.wait_ge(z_sq, 3 * t + 3)
                A(stat[:, 12 + t:13 + t], zsum[:, 2 * t + 1:2 * t + 2], ACT.Sqrt, scale=1.0 / D,
                  bias=zsum[:, 2 * TB + t:2 * TB + t + 1]).then_inc(z_sqrt, 1)

        @block.vector
        def _(dve):
            V = nc.vector

            def f(t):
                return t.bitcast(f32)

            def split_lo(u, slot):
                dve.wait_ge(w_hi_ready, split_count(u))
                V.tensor_tensor(w_lo[:, slot, :], raw[:, slot, :], f(w_hi[:, slot, :]), ALU.subtract).then_inc(w_lo_ready, 1)

            dve.wait_ge(sig_c, 1)
            V.tensor_tensor(c_act[:, :], c_act[:, :], ps[:, B_T0, 0:NB], ALU.mult).then_inc(cact, 1)
            dve.wait_ge(cact, 1)

            def softplus_step(i):
                if i == 0:
                    dve.wait_ge(sp_act, 1)
                    ins = V.tensor_scalar(sp[:, 2, :], sp[:, 1, :], 2.0, None, ALU.add)
                else:
                    dve.wait_ge(sp_step, i + 1)
                if i == 1:
                    ins = V.reciprocal(sp[:, 3, :], sp[:, 2, :])
                elif i == 2:
                    ins = V.tensor_tensor(sp[:, 2, :], sp[:, 1, :], sp[:, 3, :], ALU.mult)
                elif i == 3:
                    ins = V.tensor_tensor(sp[:, 3, :], sp[:, 2, :], sp[:, 2, :], ALU.mult)
                elif i == 4:
                    ins = V.tensor_scalar(sp[:, 4, :], sp[:, 3, :], 1.0 / 17, None, ALU.mult)
                elif 5 <= i < 12:
                    ins = V.scalar_tensor_tensor(sp[:, 4, :], sp[:, 4, :], 1.0 / (25 - 2 * i), sp[:, 3, :], ALU.add, ALU.mult)
                elif i == 12:
                    ins = V.scalar_tensor_tensor(sp[:, 4, :], sp[:, 4, :], 1.0, sp[:, 2, :], ALU.add, ALU.mult)
                elif i == 13:
                    ins = V.tensor_scalar(sp[:, 5, :], cols[:, C_LAM:C_LAM + NB], -LRU_C, 0.0, ALU.mult, ALU.max)
                elif i == 14:
                    ins = V.scalar_tensor_tensor(k_pos[:, :], sp[:, 4, :], 2.0 * LRU_C, sp[:, 5, :], ALU.mult, ALU.add)
                elif i == 15:
                    ins = V.tensor_scalar(k_neg[:, :], k_pos[:, :], -1.0, None, ALU.mult)
                ins.then_inc(sp_step, 1)

            def mod0_steps(i, steps=range(NB // 2), softplus_from=None):
                if i >= NB:
                    return
                if steps.start == 0:
                    dve.wait_ge(mod0_in[i % M0_BUFS], 32 * (i // M0_BUFS + 1))
                acc = mod0[:, :, i // 2 * 2 * P:(i // 2 + 1) * 2 * P]
                for m in steps:
                    k = i % 2 * NB // 2 + m
                    part = mod0_raw[:, i % M0_BUFS, m, :, :]
                    if k == 0:
                        V.tensor_scalar(acc, part, c_act[:, 0:1], None, ALU.mult).then_inc(mod0_acc, 1)
                    else:
                        dve.wait_ge(mod0_acc, i // 2 * NB + k)
                        V.scalar_tensor_tensor(acc, part, c_act[:, k:k + 1], acc, ALU.mult, ALU.add).then_inc(mod0_acc, 1)
                    if softplus_from is not None and softplus_from < SP_STEPS:
                        softplus_step(softplus_from + m)

            mod0_steps(0)
            dve.wait_ge(cols_sum, 1)
            V.tensor_copy(cols[:, 0:NCOL], ps[:, B_T1, 0:NCOL]).then_inc(cols_ready, 1)
            dve.wait_ge(cols_ready, 1)
            V.scalar_tensor_tensor(sp[:, 0, :], cols[:, C_LAM:C_LAM + NB], -1.0, cols[:, C_LAM:C_LAM + NB],
                                   ALU.mult, ALU.min).then_inc(sp_step, 1)
            V.tensor_scalar(cols[:, C_BC:C_BC + NB], cols[:, C_BC:C_BC + NB], 1.0, None, ALU.add).then_inc(cols_ready, 1)
            for t in range(TB):
                dve.wait_ge(x_sqrt, t + 1)
                V.reciprocal(stat[:, 8 + t:9 + t], stat[:, 4 + t:5 + t]).then_inc(x_rstd, 1)
                dve.wait_ge(x_rstd, t + 1)
                V.tensor_scalar(xs[:, t, :], xs[:, t, :], stat[:, 8 + t:9 + t], None, ALU.mult).then_inc(x_norm, 1)
            mod0_steps(1)
            dve.wait_ge(x_tr, NB)

            def evacuate(banks):
                for k in banks:
                    V.tensor_copy(xnt[:, k, :], ps[:, k, :]).then_inc(xnt_ready_dve, 1)

            evacuate((3, 6))
            dve.wait_ge(cols_ready, 2)
            for p in range(NB // 2):
                if p > 0:
                    mod0_steps(2 * p + 2, range(0, 2), softplus_from=8 * p)
                dve.wait_ge(mod0_sum, p + 1)
                k = 2 * p
                V.tensor_tensor(mcol[:, k:k + 2], ps[:, B_T1, k:k + 2], cols[:, C_BS + k:C_BS + k + 2], ALU.add).then_inc(col0_ready, 1)
                for k in (2 * p, 2 * p + 1):
                    V.scalar_tensor_tensor(s_mix[:, k:k + 1], ps[:, B_T1, NB + k:NB + k + 1], cols[:, C_BC + k:C_BC + k + 1],
                                           cols[:, C_GX + k:C_GX + k + 1], ALU.add, ALU.mult).then_inc(col0_ready, 1)
                if p == 0:
                    evacuate((4, 5))
                else:
                    mod0_steps(2 * p + 2, range(2, 4), softplus_from=8 * p)
                for k in (2 * p, 2 * p + 1):
                    if k == 1:
                        mod0_steps(2, softplus_from=0)
                    if k % 2 == 1:
                        mod0_steps(2 * p + 3, softplus_from=8 * p + 4)
                    dve.wait_ge(h_hi, k + 1)
                    V.tensor_tensor(ht_lo[:, k, :], xnt[:, k, :], f(ht_hi[:, k, :]), ALU.subtract).then_inc(h_lo, 1)
            dve.wait_ge(w_lo_ready, split_count(RING))
            split_lo(RING + 1, 1)
            dve.wait_ge(sp_step, SP_STEPS + 1)

            def diagonal_product(src, count):
                wait(dve, diag_step, 2 * count)
                V.tensor_tensor(picked, src.rearrange("p (b j) -> p b j", j=P),
                                ident[:, None, :].to_broadcast([P, HALF // P, P]), ALU.mult).then_inc(diag_step, 1)

            def diagonal_sum(dst, count):
                dve.wait_ge(diag_step, 2 * count + 1)
                V.tensor_reduce(dst, picked, AX.X, ALU.add).then_inc(diag_step, 1)

            def recurrence_gates(n):
                dve.wait_ge(i_ready, n + 1)
                V.tensor_tensor(i_t[:, :], i_t[:, :], xc[:, :], ALU.mult).then_inc(ix_ready, 1)
                dve.wait_ge(q_ready, n + 1)
                V.scalar_tensor_tensor(q_t[:, :], q_t[:, :], 1.0, t_t[:, :], ALU.add, ALU.mult).then_inc(q2_ready, 1)

            def recurrence_scan(n):
                dve.wait_ge(mult_ready, n + 1)
                dve.wait_ge(ix_ready, n + 1)
                V.tensor_tensor(i_t[:, :], i_t[:, :], q_t[:, :], ALU.mult).then_inc(bx_ready, 1)
                dve.wait_ge(bx_ready, n + 1)
                V.tensor_tensor_scan(hm[:, ds(n, 1), :].rearrange("p a n -> p (a n)"), a_t[:, :], i_t[:, :], 0.0, ALU.mult, ALU.add).then_inc(scan_ready, 1)

            def mix(n, after_conv, splits):
                first = isinstance(n, int) and n == 0
                if first:
                    dve.wait_ge(unit_done, 3)
                    dve.wait_ge(c_copied, 1)
                    V.tensor_tensor(cvp[:, KA - 1:], c_sb[:, :], ps[:, 2, :], ALU.mult).then_inc(cv_ready, 1)
                dve.wait_ge(xc_tap, n + 1)
                for k in range(KB - 1):
                    wait(dve, xc_conv, 3 * n + k)
                    V.scalar_tensor_tensor(xc[:, :], xbp[:, k:k + SEQ], cols[:, ds(C_BW + k * NB + n, 1)], xc[:, :],
                                           ALU.mult, ALU.add).then_inc(xc_conv, 1)
                if splits[0] is not None:
                    split_lo(splits[0], splits[0] % RING if isinstance(n, int) else 0)
                after_conv()
                dve.wait_ge(xc_hi_ready, n + 1)
                wait(dve, gates_done, n)
                V.tensor_tensor(xc_lo[:, :], xc[:, :], f(xc_hi[:, :]), ALU.subtract).then_inc(xc_lo_ready, 1)
                dve.wait_ge(g_hi_ready, n + 1)
                V.tensor_tensor(g_lo[:, :, :], graw[:, :, :], f(g_hi[:, :, :]), ALU.subtract).then_inc(g_lo_ready, 1)
                if not first:
                    dve.wait_ge(unit_done, 4 * n + 3)
                    dve.wait_ge(c_copied, n + 1)
                    wait(dve, ca_tap, n)
                    V.tensor_tensor(cvp[:, KA - 1:], c_sb[:, :], ps[:, 2, :], ALU.mult).then_inc(cv_ready, 1)
                if splits[1] is not None:
                    split_lo(splits[1], splits[1] % RING if isinstance(n, int) else 1)
                dve.wait_ge(ca_tap, n + 1)
                for k in range(KA - 1):
                    wait(dve, ca_conv, 2 * n + k)
                    V.scalar_tensor_tensor(ca[:, :], cvp[:, k:k + SEQ], cols[:, ds(C_AW + k * NB + n, 1)], ca[:, :],
                                           ALU.mult, ALU.add).then_inc(ca_conv, 1)
                if splits[2] is not None:
                    split_lo(splits[2], splits[2] % RING if isinstance(n, int) else 2)
                dve.wait_ge(unit_done, 4 * n + 4)
                dve.wait_ge(ca_conv, 2 * (n + 1))
                V.tensor_tensor(ca[:, :], ca[:, :], ps[:, 3, :], ALU.mult).then_inc(ya_f32, 1)
                dve.wait_ge(ya_hi_ready, n + 1)
                V.tensor_tensor(ya_lo[:, ds(n, 1), :], ca[:, None, :], f(ya_hi[:, ds(n, 1), :]), ALU.subtract).then_inc(ya_lo_ready, 1)
                if splits[3] is not None:
                    split_lo(splits[3], splits[3] % RING if isinstance(n, int) else 3)

            mix(0, lambda: None, (RING + 2, RING + 3, RING + 4, None))
            recurrence_gates(0)
            mix(1, lambda: recurrence_scan(0), (None,) + tuple(2 * RING + j for j in range(1, RING)))
            with dve.Fori(2, NB) as n:
                split_lo(4 * n + RING, 0)
                recurrence_gates(n - 1)
                mix(n, lambda: recurrence_scan(n - 1), (None,) + tuple(4 * n + RING + j for j in range(1, RING)))
            recurrence_gates(NB - 1)
            recurrence_scan(NB - 1)

            dve.wait_ge(bmod_in, 16)

            def mod_lo(n, hi):
                dve.wait_ge(mod_hi_ready, n + 1)
                V.tensor_tensor(modb_lo[:, ds(n * HALF, HALF)], modb[:, ds(n * HALF, HALF)], f(hi[:, :]),
                                ALU.subtract).then_inc(mod_lo_ready, 1)

            def gate(n, after_g):
                def mod_chunk(j):
                    dve.wait_ge(modraw_in[j % 2], 16 * (2 * n + j // 2 + 1))
                    for a in range(2):
                        wait(dve, mod_acc, 8 * n + 2 * j + a)
                        V.scalar_tensor_tensor(modb[:, ds(n * HALF, HALF)], modraw[:, j % 2, a, :],
                                               c_act[:, 2 * j + a:2 * j + a + 1], modb[:, ds(n * HALF, HALF)],
                                               ALU.mult, ALU.add).then_inc(mod_acc, 1)

                mod_chunk(0)
                dve.wait_ge(gelu_ready, n + 1)
                dve.wait_ge(scan_ready, n + 1)
                V.tensor_tensor(gel[:, None, :], gel[:, None, :], hm[:, ds(n, 1), :], ALU.mult).then_inc(yb_f32, 1)
                split_lo(U_GATE + 4 * n + 4, 0)
                after_g()
                mod_chunk(1)
                split_lo(U_GATE + 4 * n + 5, 1)
                dve.wait_ge(yb_hi_ready, n + 1)
                V.tensor_tensor(yb_lo[:, ds(n, 1), :], gel[:, None, :], f(yb_hi[:, ds(n, 1), :]), ALU.subtract).then_inc(yb_lo_ready, 1)
                mod_chunk(2)
                dve.wait_ge(unit_done, U_GATE + 4 * n + 3)
                dve.wait_ge(siga_ready, n + 1)
                V.tensor_tensor(hm[:, ds(n, 1), :], sig_a[:, None, :], ps[:, 2:3, :], ALU.mult).then_inc(m_part, 1)
                split_lo(U_GATE + 4 * n + 6, 2)
                mod_chunk(3)
                split_lo(U_GATE + 4 * n + 7, 3)

            gate(0, lambda: None)
            with dve.Fori(1, NB) as n:
                gate(n, lambda: mod_lo(n - 1, modb_hi))
            mod_lo(NB - 1, modb_hi_last)

            def w_o_lo(k):
                j = k % RING
                dve.wait_ge(w_hi_ready, wo_count(k))
                hi, lo = (wo2_hi, wo2_lo) if k < RING else (w_hi, w_lo)
                V.tensor_tensor(lo[:, j, :], raw[:, j, :], f(hi[:, j, :]), ALU.subtract).then_inc(w_lo_ready, 1)

            for n in range(NB):
                dve.wait_ge(unit_done, U_BOUT + n + 1)
                dve.wait_ge(sigb_ready, n + 1)
                V.tensor_tensor(sig_b[:, n, :], sig_b[:, n, :], ps[:, n % RING, :], ALU.mult).then_inc(bout_scaled, 1)
                if n < RING:
                    dve.wait_ge(mod_copied, 6)
                    diagonal_product(modb[:, D + n * HALF:D + (n + 1) * HALF], n)
                else:
                    w_o_lo(n - RING)
                dve.wait_ge(bout_scaled, n + 1)
                V.tensor_tensor(hm[:, n, :], hm[:, n, :], sig_b[:, n, :], ALU.add).then_inc(m_f32, 1)
                if n < RING:
                    diagonal_sum(mcol[:, NB + 4 * n:NB + 4 * n + 4], n)
                elif n == RING:
                    dve.wait_ge(gbc_in, 32)
                    dve.wait_ge(mod_copied, 8)
                    V.tensor_tensor(modb[:, 0:D], modb[:, 0:D], g_bc[:, 0, :], ALU.mult).then_inc(gm_ready, 1)
                    dve.wait_ge(diag_step, 2 * RING)
                    V.scalar_tensor_tensor(s_mlp[:, :], mcol[:, 2 * NB:3 * NB], 1.0, cols[:, C_GM:C_GM + NB],
                                           ALU.add, ALU.mult).then_inc(colf_ready, 1)
                else:
                    w_o_lo(n - 1)
                dve.wait_ge(m_hi_ready, n + 1)
                V.tensor_tensor(m_lo[:, n, :], hm[:, n, :], f(m_hi[:, n, :]), ALU.subtract).then_inc(m_lo_ready, 1)
                if n < RING:
                    split_lo(U_BOUT + n + RING, n)
            w_o_lo(NB - 1)

            dve.wait_ge(gm_ready, 1)
            dve.wait_ge(m_lo_ready, NB)
            for t in range(TB):
                for h in range(2):
                    dve.wait_ge(y_sq, 3 * t + 2 * h + 1)
                    V.tensor_tensor(y1[:, h * HALF:(h + 1) * HALF], ps[:, 2 * (t % 2) + h, :],
                                    modb[:, h * HALF:(h + 1) * HALF], ALU.mult).then_inc(y_gained, 1)
                dve.wait_ge(y_sqrt, t + 1)
                V.reciprocal(stat[:, 14:15], stat[:, 12:13]).then_inc(y_rstd, 1)
                dve.wait_ge(y_rstd, t + 1)
                dve.wait_ge(y_gained, 2 * t + 2)
                dve.wait_ge(xr_in[t], 32)
                V.scalar_tensor_tensor(xs[:, t, :], y1[:, :], stat[:, 14:15], xs[:, t, :], ALU.mult, ALU.add).then_inc(x1_ready, 1)
                if t == TB - 2:
                    split_lo(U_UP, 0)
                if t == TB - 1:
                    split_lo(U_UP + 3, 3)
                dve.wait_ge(x1_sqrt, t + 1)
                V.reciprocal(stat[:, 15:16], stat[:, 13:14]).then_inc(x1_rstd, 1)
                dve.wait_ge(x1_rstd, t + 1)
                wait(dve, xn2_tr, t)
                V.tensor_scalar(xn2[:, :], xs[:, t, :], stat[:, 15:16], None, ALU.mult).then_inc(xn2_ready, 1)
                if t == TB - 2:
                    split_lo(U_UP + 1, 1)
                    split_lo(U_UP + 2, 2)
                dve.wait_ge(xn2_tr, t + 1)
                wait(dve, h2_lo_ready, 2 * t)
                for k in range(NB // 2, NB):
                    V.tensor_scalar(h2f[:, k, :], ps[:, B_I + 2 * (t % 2), (k - NB // 2) * P:(k - NB // 2 + 1) * P],
                                    s_mlp[:, k:k + 1], mcol[:, NB + k:NB + k + 1], ALU.mult, ALU.add).then_inc(h2_f32_dve, 1)
                for part in range(2):
                    dve.wait_ge(h2_hi_ready, 2 * t + part + 1)
                    ks = slice(part * NB // 2, (part + 1) * NB // 2)
                    V.tensor_tensor(h2_lo[:, ks, t * P:(t + 1) * P], h2f[:, ks, :], f(h2_hi[:, ks, t * P:(t + 1) * P]),
                                    ALU.subtract).then_inc(h2_lo_ready, 1)
            V.tensor_tensor(modb[:, 3 * D:4 * D], modb[:, 3 * D:4 * D], g_bc[:, 1, :], ALU.mult).then_inc(gm_ready, 1)

            def up(n, j):
                dve.wait_ge(relu_ready, n + 1)
                r = relu_t[:, j % 2:j % 2 + 1, :]
                V.tensor_tensor(hid[:, ds(n, 1), :], r, r, ALU.mult).then_inc(hid_ready, 1)
                split_lo(U_UP + n + RING, j)

            def hidden_lo(n, j):
                dve.wait_ge(hd_hi_ready, n + 1)
                V.tensor_tensor(hd_lo[:, ds(j, 1), :], hid[:, ds(n, 1), :], f(hd_hi[:, ds(j, 1), :]),
                                ALU.subtract).then_inc(hd_lo_ready, 1)

            for n in range(2):
                up(n, n)
            with dve.Fori(0, FB // RING - 1) as q:
                for j in range(RING):
                    up(RING * q + j + 2, (j + 2) % RING)
            for j in range(RING):
                hidden_lo(j, j)
            for n in range(FB - 2, FB):
                up(n, n % RING)
            with dve.Fori(0, FB // RING - 1) as q:
                for j in range(RING):
                    hidden_lo(RING * q + j + RING, j)
                    split_lo(U_DOWN + RING * q + j + RING, j)
            dve.wait_ge(gm_ready, 2)
            for t in range(TB):
                for h in range(2):
                    cs = slice(h * HALF, (h + 1) * HALF)
                    dve.wait_ge(z_sq, 3 * t + 2 * h + 1)
                    wait(dve, z_out, 2 * t)
                    V.tensor_tensor(y2[:, cs], ps[:, 2 * t + h, :], modb[:, 3 * D + h * HALF:3 * D + (h + 1) * HALF],
                                    ALU.mult).then_inc(z_gained, 1)
                dve.wait_ge(z_sqrt, t + 1)
                V.reciprocal(stat[:, t:t + 1], stat[:, 12 + t:13 + t]).then_inc(z_rstd, 1)
                dve.wait_ge(z_rstd, t + 1)
                dve.wait_ge(z_gained, 2 * t + 2)
                for h in range(2):
                    cs = slice(h * HALF, (h + 1) * HALF)
                    V.scalar_tensor_tensor(xs[:, t, cs], y2[:, cs], stat[:, t:t + 1], xs[:, t, cs],
                                           ALU.mult, ALU.add).then_inc(z_out, 1)

        @block.tensor
        def _(pe):
            def column_unit(u, slot, r_hi, r_lo, bank):
                pe.wait_ge(w_lo_ready, split_count(u))
                for k in range(NB):
                    last = mm3(ps[:, bank, :], w_hi[:, slot, k * P:(k + 1) * P], w_lo[:, slot, k * P:(k + 1) * P],
                               r_hi[:, k, :], r_lo[:, k, :], k == 0, k == NB - 1)
                last.then_inc(unit_done, 1)

            pe.wait_ge(c_in, 16)
            pe.wait_ge(const_ready, 2)
            nc.tensor.transpose(ps[:, B_T0, 0:NB], crows[:, :], ident[0:NB, 0:NB]).then_inc(c_sum, 1)
            pe.wait_ge(vec_in, 16 * (len(vectors[1::3]) + len(vectors[2::3])))
            pe.wait_ge(vec_pool_in, 16 * len(vectors[0::3]))
            nc.tensor.transpose(ps[:, B_T1, 0:NCOL], vrows[0:NCOL, :], ident[0:NCOL, 0:NCOL]).then_inc(cols_sum, 1)
            pe.wait_ge(cact, 1)
            for t in range(TB):
                pe.wait_ge(x_norm, t + 1)
                for k in range(NB):
                    if t == 0 and k == B_T1:
                        pe.wait_ge(cols_ready, 1)
                    last = nc.tensor.transpose(ps[:, k, t * P:(t + 1) * P], xs[:, t, k * P:(k + 1) * P], ident[:, :])
                    if t == TB - 1:
                        last.then_inc(x_tr, 1)

            def mod0_columns(p):
                pe.wait_ge(mod0_acc, NB * (p + 1))
                for j in (2 * p, 2 * p + 1):
                    for a in range(2):
                        last = nc.tensor.matmul(ps[:, B_T1, a * NB + j:a * NB + j + 1], mod0[:, a, j * P:(j + 1) * P],
                                                ones[:, 0:1], start=True, stop=True)
                last.then_inc(mod0_sum, 1)

            pe.wait_ge(xnt_ready, 1)
            pe.wait_ge(const_ready, 3)
            mod0_columns(0)
            pe.wait_ge(xnt_ready, 4)
            pe.wait_ge(xnt_ready_dve, 1)
            for k in range(NB):
                if k % 2 == 0:
                    pe.wait_ge(w0_lo_ready, k // 2 + 1)
                pe.wait_ge(h_lo, k + 1)
                ks = slice(k * P, (k + 1) * P)
                for j in range(RING + 1):
                    if k == 0 and j == RING:
                        pe.wait_ge(xnt_ready_dve, 2)
                        pe.wait_ge(w_lo_ready, split_count(RING))
                    if k % 2 == 1 and j == 0 and k + 1 < NB:
                        mod0_columns((k + 1) // 2)
                    bank, wh, wl = (j, w0_hi[:, j, ks], w0_lo[:, j, ks]) if j < RING else (B_T0, w_hi[:, 0, ks], w_lo[:, 0, ks])
                    last = mm3(ps[:, bank, :], wh, wl, ht_hi[:, k, :], ht_lo[:, k, :], k == 0, k == NB - 1)
                    if k == NB - 1:
                        last.then_inc(unit_done, 1)

            def gates(n):
                pe.wait_ge(xc_lo_ready, n + 1)
                pe.wait_ge(g_lo_ready, n + 1)
                wait(pe, r_ready, n)
                mm3(ps[:, B_R, :], g_hi[:, 0, :], g_lo[:, 0, :], xc_hi[:, :], xc_lo[:, :], True, True)
                wait(pe, i_ready, n)
                mm3(ps[:, B_I, :], g_hi[:, 1, :], g_lo[:, 1, :], xc_hi[:, :], xc_lo[:, :], True, True).then_inc(gates_done, 1)

            def mix(n, after_xb, after_c):
                if not isinstance(n, int):
                    pe.wait_ge(xc_tap, n)
                    column_unit(4 * n, 0, ht_hi, ht_lo, 0)
                    after_xb()
                pe.wait_ge(c_copied, n)
                column_unit(4 * n + 1, 1, ht_hi, ht_lo, 1)
                after_c()
                pe.wait_ge(cv_ready, n)
                column_unit(4 * n + 2, 2, ht_hi, ht_lo, 2)
                pe.wait_ge(ya_f32, n)
                column_unit(4 * n + 3, 3, ht_hi, ht_lo, 3)

            mix(1, lambda: None, lambda: gates(0))
            with pe.Fori(2, NB) as n:
                mix(n, lambda: gates(n - 1), lambda: None)

            def gate(n, bank_sems, before, after_g, after_a):
                u = U_GATE + 4 * n
                pe.wait_ge(bank_sems[0], n + before)
                column_unit(u, 0, ht_hi, ht_lo, 0)
                after_g()
                pe.wait_ge(bank_sems[1], n + before)
                column_unit(u + 1, 1, ht_hi, ht_lo, 1)
                pe.wait_ge(bank_sems[2], n + before)
                pe.wait_ge(ya_lo_ready, NB)
                column_unit(u + 2, 2, ya_hi, ya_lo, 2)
                after_a()
                pe.wait_ge(bank_sems[3], n + before)
                column_unit(u + 3, 3, ht_hi, ht_lo, 3)

            def mod_columns(n, hi):
                pe.wait_ge(mod_lo_ready, n + 1)
                wait(pe, mod_copied, n)
                nc.tensor.matmul(ps[:, B_T0, :], ones[:, :].bitcast(f32r), hi[:, :], start=True, stop=False)
                nc.tensor.matmul(ps[:, B_T0, :], ones[:, :].bitcast(f32r), modb_lo[:, ds(n * HALF, HALF)], start=False, stop=True).then_inc(mod_sum, 1)

            gate(0, (xc_tap, c_copied, cv_ready, ya_f32), NB, lambda: gates(NB - 1), lambda: None)
            with pe.Fori(1, NB) as n:
                gate(n, (gelu_ready, siga_ready, m_part, sigb_ready), 0, lambda: None, lambda: mod_columns(n - 1, modb_hi))

            pe.wait_ge(yb_lo_ready, NB)
            for j, bank_sem in enumerate((gelu_ready, siga_ready, m_part, sigb_ready)):
                pe.wait_ge(bank_sem, NB)
                column_unit(U_BOUT + j, j, yb_hi, yb_lo, j)
                if j == 0:
                    mod_columns(NB - 1, modb_hi_last)
            with pe.Fori(1, NB // RING) as q:
                for j in range(RING):
                    pe.wait_ge(bout_scaled, RING * (q - 1) + j + 1)
                    column_unit(U_BOUT + RING * q + j, j, yb_hi, yb_lo, j)

            TR_AFTER = 5

            def transposes(t):
                pe.wait_ge(xn2_ready, t + 1)
                if t >= 2:
                    pe.wait_ge(h2_f32, NB // 2 * (t - 1))
                    pe.wait_ge(h2_f32_dve, NB // 2 * (t - 1))
                for k in range(NB):
                    last = nc.tensor.transpose(ps[:, B_R + k // 4 + 2 * (t % 2), (k % 4) * P:(k % 4 + 1) * P],
                                               xn2[:, k * P:(k + 1) * P], ident[:, :])
                last.then_inc(xn2_tr, 1)

            for t in range(TB):
                if t < 2:
                    pe.wait_ge(bout_scaled, NB - 2 + 2 * t)
                else:
                    pe.wait_ge(y_gained, 2 * (t - 1))
                order = [(k + RING) % NB for k in range(NB)] if t == TB - 1 else list(range(NB))
                for k in order:
                    if t == 0:
                        pe.wait_ge(m_lo_ready, k + 1)
                        pe.wait_ge(w_lo_ready, wo_count(k))
                    wh, wl = (wo2_hi, wo2_lo) if k < RING else (w_hi, w_lo)
                    for h in range(2):
                        cs = slice(h * HALF, (h + 1) * HALF)
                        last = mm3(ps[:, 2 * (t % 2) + h, :], m_hi[:, k, t * P:(t + 1) * P], m_lo[:, k, t * P:(t + 1) * P],
                                   wh[:, k % RING, cs], wl[:, k % RING, cs], k == order[0], k == order[-1])
                    if t == TB - 1:
                        last.then_inc(unit_done, 1)
                    if t >= 1 and k == order[TR_AFTER]:
                        transposes(t - 1)
                if t < TB - 1:
                    last.then_inc(y_done, 1)

            def up_first(j, tokens, halfway=lambda: None):
                pe.wait_ge(w_lo_ready, split_count(U_UP + j))
                for k in range(NB):
                    if k % (NB // 2) == 0:
                        pe.wait_ge(h2_lo_ready, 2 * (tokens.stop // P) - 1 + k // (NB // 2))
                    last = mm3(ps[:, j, tokens], w_hi[:, j, k * P:(k + 1) * P], w_lo[:, j, k * P:(k + 1) * P],
                               h2_hi[:, k, tokens], h2_lo[:, k, tokens], k == 0, k == NB - 1)
                    if k == NB // 2 - 1:
                        halfway()
                if tokens.start > 0:
                    last.then_inc(unit_done, 1)

            first, second = slice(0, SEQ // 2), slice(SEQ // 2, SEQ)
            up_first(0, first)
            up_first(1, first)
            pe.wait_ge(y_gained, 2 * TB)
            up_first(2, first, lambda: transposes(TB - 1))
            up_first(3, first)
            for j in range(RING):
                up_first(j, second)

            with pe.Fori(1, FB // RING) as q:
                for j in range(RING):
                    pe.wait_ge(relu_ready, RING * (q - 1) + j + 1)
                    column_unit(U_UP + RING * q + j, j, h2_hi, h2_lo, j)

            def down(slot, t, first, last, halves=range(2)):
                for h in halves:
                    cs = slice(h * HALF, (h + 1) * HALF)
                    mm = mm3(ps[:, 2 * t + h, :], hd_hi[:, slot, t * P:(t + 1) * P], hd_lo[:, slot, t * P:(t + 1) * P],
                             w_hi[:, slot, cs], w_lo[:, slot, cs], first, last)
                return mm

            def split_ready(n):
                pe.wait_ge(hd_lo_ready, n + 1)
                pe.wait_ge(w_lo_ready, split_count(U_DOWN + n))

            split_ready(0)
            for t in (2, 3, 0, 1):
                if t == 0:
                    pe.wait_ge(relu_ready, FB)
                mm = down(0, t, True, False)
            mm.then_inc(unit_done, 1)
            for n in range(1, RING):
                split_ready(n)
                for t in range(TB):
                    mm = down(n, t, False, False)
                mm.then_inc(unit_done, 1)
            with pe.Fori(1, FB // RING - 1) as q:
                for j in range(RING):
                    split_ready(RING * q + j)
                    for t in range(TB):
                        mm = down(j, t, False, False)
                    mm.then_inc(unit_done, 1)
            split_ready(FB - 2)
            for h in range(2):
                for j in range(RING - 1):
                    down(j, 0, False, False, (h,))
            split_ready(FB - 1)
            for h in range(2):
                down(RING - 1, 0, False, True, (h,)).then_inc(z_done, 1)
            for t in range(1, TB):
                for h in range(2):
                    for j in range(RING):
                        mm = down(j, t, False, j == RING - 1, (h,))
                    mm.then_inc(z_done, 1)


_INS = ['x', 'c', 'w_mod', 'b_mod', 'g_pre_mix', 'g_post_mix', 'w_in', 'conv_a_w', 'conv_a_b',
        'w_a_out', 'conv_b_w', 'conv_b_b', 'w_gate_r', 'b_gate_r', 'w_gate_i', 'b_gate_i',
        'lru_lambda', 'w_b_out', 'w_o', 'g_pre_mlp', 'g_post_mlp', 'w_mlp_up', 'w_mlp_down']
_OUTS = [((1, 512, 1024), 'float32')]


def kernel(**inputs):
    import numpy as _np
    import concourse.bacc as _bacc
    from concourse import mybir as _mybir
    from concourse.bass_utils import run_bass_kernel_spmd as _run

    nc = _bacc.Bacc("TRN2", target_bir_lowering=False, num_devices=1)
    arrays, args = {}, []
    for name in _INS:
        a = _np.ascontiguousarray(inputs[name])
        arrays[f"in_{name}_dram"] = a
        args.append(nc.dram_tensor(f"in_{name}_dram", a.shape, _mybir.dt.from_np(a.dtype), kind="ExternalInput").ap())
    for i, (shape, dtype) in enumerate(_OUTS):
        dt = _mybir.dt.from_np(_np.dtype(dtype))
        args.append(nc.dram_tensor(f"out_{i}_dram", shape, dt, kind="ExternalOutput").ap())
    hybrid_layer_kernel(nc, *args)
    r = _run(nc, [arrays], core_ids=[0])
    return r.results[0]["out_0_dram"]
```
